# Optimizing a Trainium2 kernel written in Bass

```python
import jax
import jax.numpy as jnp
from jax import lax
import numpy as np

D_MODEL = 1024
BATCH = 1
SEQ = 512
DEPTH = 2

N_EVEN = (DEPTH + 1) // 2
N_ODD = DEPTH // 2
EPS = 1e-6
NEG_INF = -1e30

SG_HEADS = 4
SG_HEAD_DIM = D_MODEL // 8
SG_WIDTH = SG_HEADS * SG_HEAD_DIM
SG_CHUNK = 128
SC_HEADS = 4
SC_HEAD_DIM = D_MODEL // 8
SC_WIDTH = SC_HEADS * SC_HEAD_DIM
CONV_WIDTH = 3
EVEN_IN = 2 * SG_WIDTH + 3 * SC_WIDTH
EVEN_MIX = SG_WIDTH + SC_WIDTH

POOL_WINDOWS = (2, 4, 8, 16)
POOL_GROUPS = len(POOL_WINDOWS)
POOL_GROUP_DIM = D_MODEL // 16
POOL_WIDTH = POOL_GROUPS * POOL_GROUP_DIM
MLA_HEADS = 6
Q_LORA = 3 * D_MODEL // 8
KV_LORA = D_MODEL // 4
QK_NOPE = 128
QK_ROPE = 64
QK_DIM = QK_NOPE + QK_ROPE
V_DIM = 128
ROPE_THETA = 10000.0
Q_BLOCK = 128
ODD_IN = POOL_WIDTH + Q_LORA + KV_LORA + QK_ROPE
ODD_MIX = POOL_WIDTH + MLA_HEADS * V_DIM

D_FF = ((8 * D_MODEL + 3 * 256 - 1) // (3 * 256)) * 256

kernel_name = 'hybrid_sgu_conv_pool_mla_trunk'

def rms_norm(x, g):
    xf = x.astype(jnp.float32)
    y = xf * lax.rsqrt(jnp.mean(xf * xf, axis=-1, keepdims=True) + EPS)
    return (y * g.astype(jnp.float32)).astype(x.dtype)

def layer_norm(x, g):
    xf = x.astype(jnp.float32)
    mu = jnp.mean(xf, axis=-1, keepdims=True)
    xc = xf - mu
    y = xc * lax.rsqrt(jnp.mean(xc * xc, axis=-1, keepdims=True) + EPS)
    return (y * g.astype(jnp.float32)).astype(x.dtype)

def spatial_gating(u, v, ln_g, w_s, b_s):
    bsz, s, _ = v.shape
    n_chunks = s // SG_CHUNK
    v = layer_norm(v.reshape(bsz, s, SG_HEADS, SG_HEAD_DIM), ln_g.reshape(SG_HEADS, SG_HEAD_DIM))
    v = v.reshape(bsz, n_chunks, SG_CHUNK, SG_HEADS, SG_HEAD_DIM)
    causal = jnp.tril(jnp.ones((SG_CHUNK, SG_CHUNK), dtype=bool))
    w = jnp.where(causal[None], w_s, 0.0).astype(v.dtype)
    mixed = jnp.einsum('hts,bnshd->bnthd', w, v) + b_s.T.astype(v.dtype)[None, None, :, :, None]
    return u * mixed.reshape(bsz, s, SG_WIDTH)

def short_conv(b_gate, c_gate, h, conv_w):
    z = c_gate * h
    y = lax.conv_general_dilated(
        z, conv_w[:, None, :].astype(z.dtype), window_strides=(1,),
        padding=[(CONV_WIDTH - 1, 0)], dimension_numbers=('NWC', 'WIO', 'NWC'),
        feature_group_count=SC_WIDTH)
    return b_gate * y

def multiscale_pool(z, lin_w, scale):
    bsz, s, _ = z.shape
    zf = z.astype(jnp.float32)
    cs = jnp.pad(jnp.cumsum(zf, axis=1), ((0, 0), (1, 0), (0, 0)))
    t = jnp.arange(1, s + 1, dtype=jnp.float32)[None, :, None]
    groups = []
    for g, w in enumerate(POOL_WINDOWS):
        lo, hi = g * POOL_GROUP_DIM, (g + 1) * POOL_GROUP_DIM
        c = cs[..., lo:hi]
        lower = jnp.pad(c[:, :s + 1 - w], ((0, 0), (w - 1, 0), (0, 0)))
        mean = (c[:, 1:] - lower) / jnp.minimum(t, float(w))
        groups.append(mean - zf[..., lo:hi])
    pooled = jnp.stack(groups, axis=2).astype(z.dtype)
    out = jnp.einsum('bsgi,gio->bsgo', pooled, lin_w)
    return out.reshape(bsz, s, POOL_WIDTH) * scale

def rope_tables(positions):
    inv_freq = ROPE_THETA ** (-jnp.arange(0, QK_ROPE, 2, dtype=jnp.float32) / QK_ROPE)
    ang = positions.astype(jnp.float32)[..., None] * inv_freq
    return jnp.cos(ang), jnp.sin(ang)

def apply_rope(x, cos, sin):
    c = cos[:, :, None, :].astype(x.dtype)
    s = sin[:, :, None, :].astype(x.dtype)
    x1, x2 = jnp.split(x, 2, axis=-1)
    return jnp.concatenate([x1 * c - x2 * s, x2 * c + x1 * s], axis=-1)

def latent_attention(q_lat, kv_lat, k_rope, cos, sin, q_a_g, q_b, kv_a_g, kv_b, q_g, k_g):
    bsz, s, _ = q_lat.shape
    q = (rms_norm(q_lat, q_a_g) @ q_b).reshape(bsz, s, MLA_HEADS, QK_DIM)
    kv = (rms_norm(kv_lat, kv_a_g) @ kv_b).reshape(bsz, s, MLA_HEADS, QK_NOPE + V_DIM)
    k_nope, v = kv[..., :QK_NOPE], kv[..., QK_NOPE:]
    k = jnp.concatenate(
        [k_nope, jnp.broadcast_to(k_rope[:, :, None, :], (bsz, s, MLA_HEADS, QK_ROPE))], axis=-1)
    q = rms_norm(q, q_g)
    k = rms_norm(k, k_g)
    q = jnp.concatenate([q[..., :QK_NOPE], apply_rope(q[..., QK_NOPE:], cos, sin)], axis=-1)
    k = jnp.concatenate([k[..., :QK_NOPE], apply_rope(k[..., QK_NOPE:], cos, sin)], axis=-1)
    scale = QK_DIM ** -0.5
    outs = []
    for i in range(s // Q_BLOCK):
        q0, k_end = i * Q_BLOCK, (i + 1) * Q_BLOCK
        logits = jnp.einsum('bqhd,bkhd->bhqk', q[:, q0:k_end], k[:, :k_end]).astype(jnp.float32) * scale
        mask = (q0 + jnp.arange(Q_BLOCK))[:, None] >= jnp.arange(k_end)[None, :]
        p = jax.nn.softmax(jnp.where(mask, logits, NEG_INF), axis=-1).astype(v.dtype)
        outs.append(jnp.einsum('bhqk,bkhd->bqhd', p, v[:, :k_end]))
    return jnp.concatenate(outs, axis=1).reshape(bsz, s, MLA_HEADS * V_DIM)

def swiglu(h, w_gate, w_up, w_down):
    return (jax.nn.silu(h @ w_gate) * (h @ w_up)) @ w_down

def setup_inputs(seed: int = 0) -> dict:
    key = jax.random.key(seed)
    k = jax.random.split(key, 23)
    f32 = jnp.float32

    def nrm(kk, shape, fan_in):
        return jax.random.normal(kk, shape, f32) * (fan_in ** -0.5)

    def gain(kk, shape, noise=0.02):
        return 1.0 + noise * jax.random.normal(kk, shape, f32)

    x = jax.random.normal(k[0], (BATCH, SEQ, D_MODEL), f32)
    positions = (jnp.arange(SEQ, dtype=jnp.int32)[None, :]
                 + jax.random.randint(k[1], (BATCH, 1), 0, SEQ, dtype=jnp.int32))
    return {
        'x': x,
        'positions': positions,
        'mix_norm': gain(k[2], (DEPTH, D_MODEL)),
        'ffn_norm': gain(k[3], (DEPTH, D_MODEL)),
        'even_w_in': nrm(k[4], (N_EVEN, D_MODEL, EVEN_IN), D_MODEL),
        'sg_ln_g': gain(k[5], (N_EVEN, SG_WIDTH)),
        'sg_w_s': nrm(k[6], (N_EVEN, SG_HEADS, SG_CHUNK, SG_CHUNK), SG_CHUNK),
        'sg_b_s': gain(k[7], (N_EVEN, SG_HEADS, SG_CHUNK), 0.1),
        'sc_conv_w': nrm(k[8], (N_EVEN, CONV_WIDTH, SC_WIDTH), CONV_WIDTH),
        'even_w_out': nrm(k[9], (N_EVEN, EVEN_MIX, D_MODEL), EVEN_MIX),
        'odd_w_in': nrm(k[10], (N_ODD, D_MODEL, ODD_IN), D_MODEL),
        'pool_w': nrm(k[11], (N_ODD, POOL_GROUPS, POOL_GROUP_DIM, POOL_GROUP_DIM), POOL_GROUP_DIM),
        'pool_scale': gain(k[12], (N_ODD, POOL_WIDTH), 0.1),
        'q_a_norm': gain(k[13], (N_ODD, Q_LORA)),
        'q_b': nrm(k[14], (N_ODD, Q_LORA, MLA_HEADS * QK_DIM), Q_LORA),
        'kv_a_norm': gain(k[15], (N_ODD, KV_LORA)),
        'kv_b': nrm(k[16], (N_ODD, KV_LORA, MLA_HEADS * (QK_NOPE + V_DIM)), KV_LORA),
        'q_norm': gain(k[17], (N_ODD, QK_DIM)),
        'k_norm': gain(k[18], (N_ODD, QK_DIM)),
        'odd_w_out': nrm(k[19], (N_ODD, ODD_MIX, D_MODEL), ODD_MIX),
        'ffn_w_gate': nrm(k[20], (DEPTH, D_MODEL, D_FF), D_MODEL),
        'ffn_w_up': nrm(k[21], (DEPTH, D_MODEL, D_FF), D_MODEL),
        'ffn_w_down': nrm(k[22], (DEPTH, D_FF, D_MODEL), D_FF),
    }

def reference(x, positions, mix_norm, ffn_norm, even_w_in, sg_ln_g, sg_w_s, sg_b_s, sc_conv_w,
              even_w_out, odd_w_in, pool_w, pool_scale, q_a_norm, q_b, kv_a_norm, kv_b, q_norm,
              k_norm, odd_w_out, ffn_w_gate, ffn_w_up, ffn_w_down):
    cos, sin = rope_tables(positions)
    for layer in range(DEPTH):
        i = layer // 2
        h = rms_norm(x, mix_norm[layer])
        if layer % 2 == 0:
            proj = h @ even_w_in[i]
            u, v, b_gate, c_gate, hv = jnp.split(
                proj, [SG_WIDTH, 2 * SG_WIDTH, 2 * SG_WIDTH + SC_WIDTH, 2 * SG_WIDTH + 2 * SC_WIDTH], axis=-1)
            a_out = spatial_gating(jax.nn.gelu(u, approximate=False), jax.nn.gelu(v, approximate=False),
                                   sg_ln_g[i], sg_w_s[i], sg_b_s[i])
            b_out = short_conv(b_gate, c_gate, hv, sc_conv_w[i])
            x = x + jnp.concatenate([a_out, b_out], axis=-1) @ even_w_out[i]
        else:
            proj = h @ odd_w_in[i]
            z_pool, q_lat, kv_lat, k_rope = jnp.split(
                proj, [POOL_WIDTH, POOL_WIDTH + Q_LORA, POOL_WIDTH + Q_LORA + KV_LORA], axis=-1)
            c_out = multiscale_pool(z_pool, pool_w[i], pool_scale[i])
            d_out = latent_attention(q_lat, kv_lat, k_rope, cos, sin, q_a_norm[i], q_b[i],
                                     kv_a_norm[i], kv_b[i], q_norm[i], k_norm[i])
            x = x + jnp.concatenate([c_out, d_out], axis=-1) @ odd_w_out[i]
        h = rms_norm(x, ffn_norm[layer])
        x = x + swiglu(h, ffn_w_gate[layer], ffn_w_up[layer], ffn_w_down[layer])
    return x


_drawn_inputs = setup_inputs


def setup_inputs(seed=0):
    import zlib

    import numpy as np

    out = dict(_drawn_inputs(seed))
    spreads = {}
    factors = {'ffn_norm': 3.616,
     'sg_ln_g': 8.0,
     'q_a_norm': 8.0,
     'kv_a_norm': 8.0,
     'q_norm': 8.0,
     'k_norm': 8.0,
     'pool_scale': 8.0}
    for name, (base, spread) in spreads.items():
        noise = np.random.default_rng([zlib.crc32(name.encode()), seed]).standard_normal(out[name].shape)
        drawn = base * np.exp(spread * noise) if base else spread * noise
        out[name] = jnp.asarray(drawn.astype(out[name].dtype))
    for name, factor in factors.items():
        out[name] = (out[name] * factor).astype(out[name].dtype)
    return out
```

```python
from contextlib import ExitStack

import concourse.bass as bass
from concourse import mybir

F32 = mybir.dt.float32
F32R = mybir.dt.float32r
I32 = mybir.dt.int32
ACT = mybir.ActivationFunctionType
ALU = mybir.AluOpType
AX = mybir.AxisListType

P = 128
T = 512
TT = T // P
D = 1024
KC = D // P
EPS = 1e-6
NEG = -1e30
FF = 2816
HC = FF // P // 2
HEADS = 6
PAIRS = HEADS // 2
QK = 192
QC, KVC = 3, 2
SM_SCALE = QK ** -0.5

U_EIN, U_EOUT, U_F0 = 0, 10, 14
U_OIN, U_PAIR, U_OOUT, U_F1 = 52, 56, 59, 63
N_UNITS = 101
HALF_UNITS = HC + KC

H_EIN, H_EOUT, H_F0, H_OIN, H_OOUT, H_F1 = 0, 8, 12, 34, 38, 42

W_UNIT = 2 * KC * P
W_DOWN = HC * P
W_LAST_IN = KC * 2 * P
W_PAIR = QC * 3 * P + KVC * 2 * P + KVC * 2 * P
SLOT = max(W_UNIT, W_PAIR)

C_MIX, C_FFN, C_CONV, C_PSCALE, C_LAT, C_QG, C_QGR, C_KG, C_KGR, C_INVF, C_POOLW, C_POOLFIX, N_COLS = (
    0, 16, 32, 44, 46, 51, 52, 53, 54, 55, 56, 58, 90)
S_RV, S_SUM, S_MEAN, S_VAR, S_VR, S_LAT, S_RQ2, S_Q, S_SF, S_MX, S_NB, S_RS, S_RI, S_PI, S_ONE = (
    0, 4, 20, 36, 52, 68, 80, 84, 92, 100, 104, 108, 112, 116, 118)


EVEN_ORDER = [("c", 0), ("h", 0), ("b", 0), ("c", 1), ("h", 1), ("b", 1),
              ("c", 2), ("h", 2), ("b", 2), ("c", 3), ("h", 3), ("b", 3)]
ATTENTION = ([("S", 0, 0), ("S", 0, 1), ("S", 0, 2), ("S", 0, 3), ("T", 0, 0), ("T", 0, 1), ("S", 1, 0), ("T", 0, 2),
              ("S", 1, 1), ("T", 0, 3), ("S", 1, 2), ("V", 0, 0), ("S", 1, 3)]
             + [("T", 1, i) for i in range(4)] + [("V", 1, 0)])


def unit_width(n):
    for base in (U_F0, U_F1):
        if base <= n < base + 2 * HALF_UNITS:
            return W_UNIT if (n - base) % HALF_UNITS < HC else W_DOWN
    if U_PAIR <= n < U_OOUT:
        return W_PAIR
    return W_UNIT


def trunk(nc, xT, pos, cols_d, sg_g, sg_b, sg_w, pool_w, w_ein, w_eout, w_oin, w_pair, w_oout, w_gu, w_dn, out):
    with ExitStack() as ctx:
        def sem(name):
            return ctx.enter_context(nc.semaphore(name))

        here = [nc.sbuf_base + 31 & ~31]

        def at(name, shape, dt, offset):
            return nc.alloc_sbuf_tensor_at(name, shape, dt, offset=offset)

        def sb(name, shape, dt=F32):
            n = 4
            for s in shape[1:]:
                n *= s
            off = here[0]
            here[0] += n + 31 & ~31
            return at(name, shape, dt, off), off

        x, _ = sb("x", [P, KC, T])
        gxh, gx_at = sb("gxh", [P, KC, T], F32R)
        gxl, _ = sb("gxl", [P, KC, T], F32R)
        hidh, hidh_at = sb("hidh", [P, HC, T], F32R)
        hidl, hidl_at = sb("hidl", [P, HC, T], F32R)
        mixh, mixl = hidh, hidl
        raw = [sb(f"raw{i}", [P, SLOT])[0] for i in range(2)]
        wh = [sb(f"wh{i}", [P, SLOT], F32R)[0] for i in range(2)]
        wl = [sb(f"wl{i}", [P, SLOT], F32R)[0] for i in range(2)]
        rstd, _ = sb("rstd", [P, T])
        acc, _ = sb("acc", [P, T])
        gate_s, gate_at = sb("gate_s", [P, T])
        up_s, up_at = sb("up_s", [P, T])
        cosT, _ = sb("cosT", [P, T])
        sinT, _ = sb("sinT", [P, T])
        ident, _ = sb("ident", [P, P])
        identr, _ = sb("identr", [P, P], F32R)
        mask, _ = sb("mask", [P, P])
        maskr, _ = sb("maskr", [P, P], F32R)
        ones, _ = sb("ones", [P, P])
        half_rows, _ = sb("half_rows", [P, 2])
        cols, _ = sb("cols", [P, N_COLS])
        sm, _ = sb("sm", [P, 128])
        pwr, _ = sb("pwr", [P, 2, P])
        mixer_at = here[0]

        gv, gv_at = sb("gv", [P, TT, T])
        vnh, _ = sb("vnh", [P, TT, T], F32R)
        vnl, _ = sb("vnl", [P, TT, T], F32R)
        mixed, _ = sb("mixed", [P, 4, T])
        wsr, _ = sb("wsr", [P, 4, P])
        wsh, _ = sb("wsh", [P, 4, P], F32R)
        wsl, _ = sb("wsl", [P, 4, P], F32R)
        bbc, _ = sb("bbc", [P, 4, P])
        lng, _ = sb("lng", [P, T])
        cb, _ = sb("cb", [P, T])
        z, _ = sb("z", [P, T + 2])
        y, _ = sb("y", [P, T])
        assert here[0] <= nc.sbuf_usable_end, here[0]

        posi = at("posi", [P, T], I32, gv_at)
        ang = at("ang", [P, T], F32, gv_at + 4 * T)
        turn = at("turn", [P, T], F32, gv_at + 8 * T)
        hsin = at("hsin", [P, T], F32, gv_at + 12 * T)

        here[0] = mixer_at
        lat, lat_at = sb("lat", [P, 6, T])
        lath, _ = sb("lath", [P, 5, T], F32R)
        latl, _ = sb("latl", [P, 5, T], F32R)
        rk = acc
        ptm, pt_at = sb("ptm", [P, 2 * TT * T])
        assert here[0] <= nc.sbuf_usable_end, here[0]
        pth = at("pth", [P, TT, T], F32R, pt_at)
        ptl = at("ptl", [P, TT, T], F32R, pt_at + 4 * TT * T)
        PADW = T + 15
        zp = [at(f"zp{c}", [P, PADW], F32, pt_at + c * 2112) for c in range(2)]
        win = [at(f"win{c}", [P, PADW], F32, pt_at + 4224 + c * 2112) for c in range(2)]
        pm = [at(f"pm{c}", [P, T], F32, pt_at + 8448 + c * 4 * T) for c in range(2)]
        pwh = at("pwh", [P, 2, P], F32R, pt_at + 12544)
        pwl = at("pwl", [P, 2, P], F32R, pt_at + 13568)
        sq = at("sq", [P, 2, T], F32, lat_at)
        sqr = at("sqr", [P, T], F32, lat_at + 8 * T)
        qx = at("qx", [P, T], F32, lat_at + 12 * T)
        qrot = at("qrot", [P, T], F32, lat_at + 16 * T)
        krp = at("krp", [P, T], F32, lat_at + 20 * T)
        fk = at("fk", [P, 2, T], F32, gate_at)
        assert up_at == gate_at + 4 * T
        prob = [at(f"prob{i}", [P, T], F32, hidh_at + (8 + i) * 4 * T) for i in range(3)]
        acckv = at("acckv", [P, T], F32, hidh_at + 10 * 4 * T)
        rkv = rstd
        kk = at("kk", [P, 2, T], F32, hidl_at + 8 * 4 * T)
        krsq = at("krsq", [P, T], F32, hidl_at + 10 * 4 * T)
        G = gx_at
        qnh = at("qnh", [P, 2, T], F32R, G)
        qnl = at("qnl", [P, 2, T], F32R, G + 8 * T)
        knh = at("knh", [P, 2, T], F32R, G + 16 * T)
        knl = at("knl", [P, 2, T], F32R, G + 24 * T)
        qrh = at("qrh", [P, T], F32R, G + 32 * T)
        qrl = at("qrl", [P, T], F32R, G + 36 * T)
        krh = at("krh", [P, T], F32R, G + 40 * T)
        krl = at("krl", [P, T], F32R, G + 44 * T)
        vh = at("vh", [P, TT, 2 * P], F32R, G + 48 * T)
        vl = at("vl", [P, TT, 2 * P], F32R, G + 56 * T)

        bank = [ctx.enter_context(nc.psum_tensor(f"bank{i}", [P, T], F32)) for i in range(8)]

        x_landed = [sem(f"x_landed{c}") for c in range(KC)]
        cols_landed = sem("cols_landed")
        consts_landed = sem("consts_landed")
        raw_landed = [sem("raw_landed0"), sem("raw_landed1")]
        split_hi = sem("split_hi")
        split_lo = sem("split_lo")
        half_ready = sem("half_ready")
        unit_used = sem("unit_used")
        out_read = sem("out_read")
        x_done = sem("x_done")
        gx_hi = sem("gx_hi")
        gx_lo = sem("gx_lo")
        sumsq = sem("sumsq")
        norm_mm = sem("norm_mm")
        norm_done = sem("norm_done")
        silu_done = sem("silu_done")
        prod_done = sem("prod_done")
        hid_hi = sem("hid_hi")
        hid_lo = sem("hid_lo")
        pool_ready = sem("pool_ready")
        pool_chain = sem("pool_chain")
        dve_chain = sem("dve_chain")
        act_chain = sem("act_chain")
        vconst = sem("vconst")
        aconst = sem("aconst")
        v_gelu = sem("v_gelu")
        v_stat = sem("v_stat")
        v_rs = sem("v_rs")
        v_norm = sem("v_norm")
        v_hi = sem("v_hi")
        v_lo = sem("v_lo")
        mix_mm = sem("mix_mm")
        mix_read = sem("mix_read")
        mx_f = sem("mx_f")
        mx_hi = sem("mx_hi")
        mx_lo = sem("mx_lo")
        u_gelu = sem("u_gelu")
        lat_hi = sem("lat_hi")
        lat_lo = sem("lat_lo")
        lat_sq = sem("lat_sq")
        lat_mm = sem("lat_mm")
        lat_r = sem("lat_r")
        rk_done = sem("rk_done")
        pooled = sem("pooled")
        pooled_hi = sem("pooled_hi")
        pooled_lo = sem("pooled_lo")
        pw_lo = sem("pw_lo")
        pool_mm = sem("pool_mm")
        sf_done = sem("sf_done")
        proj = sem("proj")
        proj_read = sem("proj_read")
        proj_sq = sem("proj_sq")
        proj_hi = sem("proj_hi")
        q_rot = sem("q_rot")
        pair_lo = sem("pair_lo")
        k_r = sem("k_r")
        k_f = sem("k_f")
        k_hi = sem("k_hi")
        q_r = sem("q_r")
        score = sem("score")
        score_max = sem("score_max")
        prob_exp = sem("prob_exp")
        row_recip = sem("row_recip")
        prob_n = sem("prob_n")
        prob_t = sem("prob_t")
        pt_hi = sem("pt_hi")
        pt_lo = sem("pt_lo")
        pv = sem("pv")
        stored = sem("stored")

        block = ctx.enter_context(nc.Block())

        def col(c):
            return cols[:, c:c + 1]

        @block.sync
        def _(sp):
            def load(n, src, width):
                if n >= 2:
                    sp.wait_ge(split_lo, 2 * (n - 1))
                sp.dma_start(raw[n % 2][:, 0:width], src).then_inc(raw_landed[n % 2], 16)

            def load_loop(n0, count, src, width):
                assert count % 2 == 0
                with sp.Fori(0, count // 2) as i:
                    for j in range(2):
                        sp.wait_ge(split_lo, 4 * i + 2 * (n0 + j - 1))
                        sp.dma_start(raw[(n0 + j) % 2][:, 0:width],
                                     src(2 * i + j)).then_inc(raw_landed[(n0 + j) % 2], 16)

            def ffn(layer, base):
                for half in range(2):
                    n = base + half * HALF_UNITS
                    load(n, w_gu[layer, half * HC], W_UNIT)
                    load_loop(n + 1, HC - 1,
                              lambda i: w_gu[layer, bass.ds(half * HC + 1 + i, 1)].rearrange("a p w -> p (a w)"),
                              W_UNIT)
                    load_loop(n + HC, KC,
                              lambda i: w_dn[layer, bass.ds(half * KC + i, 1)].rearrange("a p w -> p (a w)"), W_DOWN)

            for k in range(10):
                load(U_EIN + k, w_ein[k], W_UNIT)
            for k in range(4):
                load(U_EOUT + k, w_eout[k], W_UNIT)
            ffn(0, U_F0)
            for k in range(4):
                load(U_OIN + k, w_oin[k], W_UNIT)
            for k in range(PAIRS):
                load(U_PAIR + k, w_pair[k], W_PAIR)
            for k in range(4):
                load(U_OOUT + k, w_oout[k], W_UNIT)
            ffn(1, U_F1)
            for m in range(KC):
                sp.wait_ge(x_done, 3 * KC + m + 1)
                sp.dma_start(out[:, m, :], x[:, m, :]).then_inc(stored, 16)
            sp.wait_ge(stored, 16 * KC)

        @block.gpsimd
        def _(pool):
            links = [0]

            def link(ins):
                links[0] += 1
                ins.then_inc(pool_chain, 1)
                pool.wait_ge(pool_chain, links[0])

            link(pool.memset(ident[:], 0.0))
            pool.affine_select(out=ident[:], in_=ident[:], compare_op=ALU.not_equal, fill=1.0, base=0,
                               pattern=[[-1, P]], channel_multiplier=1).then_inc(pool_ready, 1)
            link(pool.memset(mask[:], 0.0))
            pool.affine_select(out=mask[:], in_=mask[:], compare_op=ALU.is_ge, fill=NEG, base=0,
                               pattern=[[-1, P]], channel_multiplier=1).then_inc(pool_ready, 1)
            pool.wait_ge(consts_landed, 16 * 8)
            pool.affine_select(out=wsr[:], in_=wsr[:], compare_op=ALU.is_ge, fill=0.0, base=0,
                               pattern=[[0, 4], [1, P]], channel_multiplier=-1).then_inc(pool_ready, 1)

            def residual_sumsq(ready, sqx):
                for c in range(KC):
                    ready(c)
                    if c == 0:
                        link(pool.tensor_tensor(acc[:], x[:, c, :], x[:, c, :], ALU.mult))
                    else:
                        link(pool.tensor_tensor(sqx, x[:, c, :], x[:, c, :], ALU.mult))
                        ins = pool.tensor_tensor(acc[:], acc[:], sqx, ALU.add)
                        if c < KC - 1:
                            link(ins)
                        else:
                            ins.then_inc(sumsq, 1)

            residual_sumsq(lambda c: pool.wait_ge(x_landed[c], 16), y[:])
            residual_sumsq(lambda c: pool.wait_ge(out_read, 2 * H_EOUT + c + 1), cb[:])
            residual_sumsq(lambda c: pool.wait_ge(x_done, KC + c + 1), cb[:])

            for i in range(3):
                pool.wait_ge(out_read, 2 * H_OIN + i + 1)
                if i == 0:
                    pool.wait_ge(norm_mm, 4)
                    link(pool.tensor_tensor(acc[:], lat[:, 0, :], lat[:, 0, :], ALU.mult))
                else:
                    link(pool.tensor_tensor(krsq[:], lat[:, i, :], lat[:, i, :], ALU.mult))
                    link(pool.tensor_tensor(acc[:], acc[:], krsq[:], ALU.add))
            pool.wait_ge(out_read, 2 * H_OIN + 4)
            link(pool.tensor_tensor(acckv[:], lat[:, 3, :], lat[:, 3, :], ALU.mult))
            pool.wait_ge(out_read, 2 * H_OIN + 5)
            link(pool.tensor_tensor(krsq[:], lat[:, 4, :], lat[:, 4, :], ALU.mult))
            link(pool.tensor_tensor(acckv[:], acckv[:], krsq[:], ALU.add))
            pool.wait_ge(out_read, 2 * H_OIN + 6)
            pool.tensor_tensor(krsq[:], lat[:, 5, :], lat[:, 5, :], ALU.mult).then_inc(lat_sq, 1)

            for c in range(2):
                pool.wait_ge(out_read, 2 * H_OIN + 7 + c)
                src, width, lo = zp[c], 1, 0
                for s in range(2 * c + 2):
                    dst = win[s % 2]
                    lo = 2 * width - 1
                    link(pool.tensor_tensor(dst[:, lo:], src[:, lo:], src[:, lo - width:PADW - width], ALU.add))
                    src, width = dst, 2 * width
                half = win[(2 * c) % 2]
                full = win[(2 * c + 1) % 2]
                link(pool.tensor_scalar(pm[c][0:64, :], half[0:64, 15:], cols[0:64, C_POOLW + c:C_POOLW + c + 1], None,
                                        ALU.mult))
                link(pool.tensor_scalar(pm[c][64:P, :], full[64:P, 15:], cols[64:P, C_POOLW + c:C_POOLW + c + 1], None,
                                        ALU.mult))
                link(pool.tensor_tensor(pm[c][:, 0:16], pm[c][:, 0:16], cols[:, C_POOLFIX + 16 * c:C_POOLFIX + 16 * c + 16],
                                        ALU.mult))
                pool.tensor_tensor(pm[c][:], pm[c][:], zp[c][:, 15:], ALU.subtract).then_inc(pooled, 1)

            for p in range(PAIRS):
                for what, hd, i in ATTENTION:
                    if what == "S":
                        q = 4 * (2 * p + hd) + i
                        pool.wait_ge(row_recip, q + 1)
                        t = prob[q % 3][:, 0:P * (i + 1)]
                        pool.tensor_scalar(t, t, sm[:, S_RI + i:S_RI + i + 1], None, ALU.mult).then_inc(prob_n, 1)

            residual_sumsq(lambda c: pool.wait_ge(out_read, 2 * H_OOUT + c + 1), gate_s[:])

        @block.scalar
        def _(act):
            links = [0]

            def link(ins):
                links[0] += 1
                ins.then_inc(act_chain, 1)
                act.wait_ge(act_chain, links[0])

            act.dma_start(cols[:], cols_d).then_inc(cols_landed, 16)
            for c in range(KC):
                act.dma_start(x[:, c, :], xT[:, c, :]).then_inc(x_landed[c], 16)
            act.wait_ge(vconst, 1)
            for c in range(2):
                for g in range(2):
                    act.dma_start(pwr[64 * g:64 * g + 64, c, 64 * g:64 * g + 64],
                                  pool_w[2 * c + g]).then_inc(consts_landed, 16)
            act.dma_start(posi[:], pos.broadcast_to([P, T])).then_inc(consts_landed, 16)
            act.dma_start(wsr[:], sg_w).then_inc(consts_landed, 16)
            act.dma_start(bbc[:].rearrange("p a b -> p (a b)"), sg_b.broadcast_to([P, T])).then_inc(consts_landed, 16)
            act.dma_start(lng[:], sg_g.broadcast_to([P, T])).then_inc(consts_landed, 16)

            def split(n, i=None, slot=None):
                s = n % 2
                w = unit_width(n)
                if i is None:
                    act.wait_ge(raw_landed[s], 16 * (n // 2 + 1))
                    if n >= 2:
                        act.wait_ge(unit_used, n - 1)
                else:
                    act.wait_ge(raw_landed[s], 16 * i + 16 * (n // 2 + 1))
                    act.wait_ge(unit_used, 2 * i + n - 1)
                for a, b in ((0, w // 2), (w // 2, w)):
                    act.activation(wh[s][:, a:b], raw[s][:, a:b], ACT.Copy).then_inc(split_hi, 1)

            def rsqrt(dst, src, scale):
                link(act.activation(dst, src, ACT.Ln, bias=sm[:, S_ONE + 1:S_ONE + 2], scale=scale))
                return act.activation(dst, dst, ACT.Exp, scale=-0.5)

            def norm(k):
                act.wait_ge(norm_mm, k)
                rsqrt(rstd[:], bank[6][:, :], 1.0 / D).then_inc(norm_done, 1)

            def gx(c, g):
                act.activation(gxh[:, c, :], x[:, c, :], ACT.Copy, scale=col(g + c)).then_inc(gx_hi, 1)

            def gate_step(n, h, i=None):
                k = 0 if i is None else 2 * i
                g = h - H_F0 if h < H_OIN else h - H_F1 + 2 * HC
                c = (g % HC) + k
                act.wait_ge(out_read, 2 * k + 2 * h + 1)
                act.activation(gate_s[:], gate_s[:], ACT.Silu).then_inc(silu_done, 1)
                act.wait_ge(prod_done, k + g + 1)
                dst = hidh[:, c, :] if i is None else hidh[:, bass.ds(c, 1), :].rearrange("p a t -> p (a t)")
                act.activation(dst, gate_s[:], ACT.Copy).then_inc(hid_hi, 1)

            def down_gx(g, k, m, i=None):
                if i is None:
                    act.wait_ge(x_done, k + m + 1)
                    gx(m, g)
                else:
                    act.wait_ge(x_done, 2 * i + k + m + 1)
                    mm = 2 * i + m
                    act.activation(gxh[:, bass.ds(mm, 1), :].rearrange("p a t -> p (a t)"),
                                   x[:, bass.ds(mm, 1), :].rearrange("p a t -> p (a t)"), ACT.Copy,
                                   scale=cols[:, bass.ds(g + mm, 1)]).then_inc(gx_hi, 1)

            def ffn(base, hbase, layer, gain_next):
                for half in range(2):
                    n, h = base + half * HALF_UNITS, hbase + half * HC
                    if half == 0:
                        norm(2 * layer + 3)
                    gate_step(n, h)
                    split(n + 2)
                    with act.Fori(0, 4) as i:
                        for j in range(2):
                            gate_step(n + 1 + j, h + 1 + j, i)
                            split(n + 3 + j, i)
                    for c in range(9, 11):
                        gate_step(n + c, h + c)
                        split(n + c + 2)
                    k = (2 * layer + half) * KC
                    n += HC
                    with act.Fori(0, 3) as i:
                        for j in range(2):
                            if half == 1 and gain_next is not None:
                                down_gx(gain_next, k, j, i)
                            split(n + 2 + j, i)
                    for m in range(6, 8):
                        if half == 1 and gain_next is not None:
                            down_gx(gain_next, k, m)
                        if n + m + 2 < N_UNITS:
                            split(n + m + 2)

            act.wait_ge(cols_landed, 16)
            for c in range(KC):
                act.wait_ge(x_landed[c], 16)
                gx(c, C_MIX)
                if c == 1:
                    split(0)
            split(1)
            act.wait_ge(pool_ready, 3)
            act.activation(identr[:], ident[:], ACT.Copy)
            act.activation(maskr[:], mask[:], ACT.Copy)
            act.activation(wsh[:], wsr[:], ACT.Copy).then_inc(aconst, 1)
            act.wait_ge(vconst, 2)
            act.activation(hsin[:], ang[:], ACT.Sin, scale=0.5)
            act.activation(turn[:], ang[:], ACT.Sin).then_inc(aconst, 1)

            norm(1)
            act.wait_ge(norm_mm, 2)
            rsqrt(sm[:, S_RV:S_RV + TT], bank[7][:, 0:TT], 1.0 / D).then_inc(norm_done, 1)
            act.wait_ge(norm_done, 2)
            act.wait_ge(unit_used, 2)
            split(2)
            act.wait_ge(vconst, 3)
            for t in range(TT):
                act.activation(gv[:, t, :], bank[t][:, :], ACT.Gelu,
                               scale=sm[:, S_RV + t:S_RV + t + 1]).then_inc(v_gelu, 1)
            split(3)
            act.wait_ge(v_stat, 1)
            rsqrt(sm[:, S_VR:S_VR + 16], sm[:, S_VAR:S_VAR + 16], 1.0).then_inc(v_rs, 1)
            act.wait_ge(v_norm, 1)
            act.activation(vnh[:], gv[:], ACT.Copy).then_inc(v_hi, 1)
            gates = 0
            for k in range(2, 8):
                split(k + 2)
                for kind, j in EVEN_ORDER[2 * (k - 2):2 * (k - 2) + 2]:
                    if kind == "b":
                        gates += 1
                        act.wait_ge(mx_f, gates)
                        act.activation(mixh[:, 4 + j, :], up_s[:], ACT.Copy).then_inc(mx_hi, 1)
            for k in range(8, 10):
                for o in range(2):
                    j = 2 * (k - 8) + o
                    act.wait_ge(out_read, 2 * (H_EIN + k - 2) + o + 1)
                    act.activation(gate_s[:], gate_s[:], ACT.Gelu).then_inc(u_gelu, 1)
                    act.wait_ge(mx_f, 5 + j)
                    act.activation(mixh[:, j, :], up_s[:], ACT.Copy).then_inc(mx_hi, 1)
                split(k + 2)
            for k in range(4):
                for o in range(2):
                    act.wait_ge(out_read, 2 * (H_EOUT + k) + o + 1)
                    gx(2 * k + o, C_FFN)
                split(U_EOUT + k + 2)

            ffn(U_F0, H_F0, 0, C_MIX + KC)

            norm(4)
            for k in range(4):
                for o in range(2):
                    i = 2 * k + o
                    if i < 5:
                        act.wait_ge(out_read, 2 * H_OIN + i + 1)
                        act.activation(lath[:, i, :], lat[:, i, :], ACT.Copy, scale=col(C_LAT + i)).then_inc(lat_hi, 1)
                split(U_OIN + k + 2)
            act.wait_ge(lat_mm, 1)
            link(act.activation(sm[:, S_LAT:S_LAT + 4], bank[6][:, 0:4], ACT.Ln, bias=sm[:, S_ONE + 1:S_ONE + 2],
                                scale=1.0 / (QC * P)))
            link(act.activation(sm[:, S_LAT + 4:S_LAT + 8], bank[6][:, 4:8], ACT.Ln, bias=sm[:, S_ONE + 1:S_ONE + 2],
                                scale=1.0 / (KVC * P)))
            act.activation(sm[:, S_LAT:S_LAT + 8], sm[:, S_LAT:S_LAT + 8], ACT.Exp, scale=-0.5).then_inc(lat_r, 1)
            act.wait_ge(out_read, 2 * H_OIN + 8)
            rsqrt(rkv[:], bank[7][:, :], 1.0 / (KVC * P)).then_inc(lat_r, 1)
            act.wait_ge(lat_r, 2)
            act.activation(pwh[:], pwr[:], ACT.Copy).then_inc(aconst, 1)

            for p in range(PAIRS):
                b = 10 * p
                if p == 0:
                    act.wait_ge(lat_lo, 5)
                    act.wait_ge(lat_sq, 1)
                    act.wait_ge(rk_done, 1)
                for o in range(2):
                    act.wait_ge(proj, b + o + 1)
                    act.activation(sq[:, o, :], bank[(b + o) % 3][:, :], ACT.Square).then_inc(proj_sq, 1)
                    act.activation(qnh[:, o, :], bank[(b + o) % 3][:, :], ACT.Copy,
                                   scale=col(C_QG)).then_inc(proj_hi, 1)
                act.wait_ge(proj, b + 3)
                act.activation(sqr[:], bank[(b + 2) % 3][:, :], ACT.Square).then_inc(proj_sq, 1)
                act.wait_ge(proj_read, 8 * p + 4)
                rsqrt(sm[:, S_Q:S_Q + 8], sm[:, S_Q:S_Q + 8], 1.0 / QK).then_inc(q_r, 1)
                for o in range(2):
                    act.wait_ge(proj_read, 8 * p + 5 + o)
                    act.activation(sq[:, o, :], kk[:, o, :], ACT.Square).then_inc(proj_sq, 1)
                act.wait_ge(q_rot, p + 1)
                act.activation(qrh[:], qx[:], ACT.Copy).then_inc(proj_hi, 1)
                for o in range(2):
                    act.wait_ge(proj, b + 7 + o)
                    for t in range(2):
                        tt = 2 * o + t
                        act.activation(vh[:, tt, :], bank[(b + 6 + o) % 3][:, t * 256:t * 256 + 256], ACT.Copy,
                                       scale=sm[:, S_LAT + 4 + tt:S_LAT + 5 + tt]).then_inc(proj_hi, 1)
                for o in range(2):
                    act.wait_ge(proj, b + 9 + o)
                    rsqrt(fk[:, o, :], bank[(b + 8 + o) % 3][:, :], 1.0 / QK).then_inc(k_r, 1)
                for o in range(2):
                    act.wait_ge(k_f, 3 * p + o + 1)
                    act.activation(knh[:, o, :], kk[:, o, :], ACT.Copy).then_inc(k_hi, 1)
                act.wait_ge(k_f, 3 * p + 3)
                act.activation(krh[:], krp[:], ACT.Copy).then_inc(k_hi, 1)
                split(U_PAIR + p + 2)
                if p == 0:
                    for c in range(2):
                        act.wait_ge(pooled, c + 1)
                        act.activation(mixh[:, 2 + c, :], pm[c][:], ACT.Copy).then_inc(pooled_hi, 1)
                    for c in range(2):
                        act.wait_ge(pool_mm, c + 1)
                        act.activation(mixh[:, c, :], bank[5 + c][:, :], ACT.Copy,
                                       scale=col(C_PSCALE + c)).then_inc(mx_hi, 1)
                for what, hd, i in ATTENTION:
                    head = 2 * p + hd
                    q = 4 * head + i
                    if what == "S":
                        act.wait_ge(score_max, q + 1)
                        if q >= 3:
                            act.wait_ge(prob_t, q - 2)
                        act.activation(prob[q % 3][:, 0:P * (i + 1)], bank[3 + q % 2][:, 0:P * (i + 1)], ACT.Exp,
                                       bias=sm[:, S_NB + i:S_NB + i + 1],
                                       scale=sm[:, S_SF + 4 * hd + i:S_SF + 4 * hd + i + 1],
                                       accum_out=sm[:, S_RS + i:S_RS + i + 1]).then_inc(prob_exp, 1)
                    elif what == "T":
                        act.wait_ge(prob_t, q + 1)
                        act.activation(pth[:, 0:i + 1, P * i:P * i + P],
                                       bank[5 + q % 2][:, 0:P * (i + 1)].rearrange("p (j q) -> p j q", q=P),
                                       ACT.Copy).then_inc(pt_hi, 1)
                    else:
                        act.wait_ge(pv, head + 1)
                        act.activation(mixh[:, 2 + head, :], bank[7][:, :], ACT.Copy).then_inc(mx_hi, 1)

            for k in range(4):
                for o in range(2):
                    act.wait_ge(out_read, 2 * (H_OOUT + k) + o + 1)
                    gx(2 * k + o, C_FFN + KC)
                split(U_OOUT + k + 2)
            ffn(U_F1, H_F1, 1, None)

        @block.vector
        def _(dve):
            links = [0]

            def link(ins):
                links[0] += 1
                ins.then_inc(dve_chain, 1)
                dve.wait_ge(dve_chain, links[0])

            def split(n, i=None):
                s = n % 2
                w = unit_width(n)
                for k, (a, b) in enumerate(((0, w // 2), (w // 2, w))):
                    if i is None:
                        dve.wait_ge(split_hi, 2 * n + k + 1)
                    else:
                        dve.wait_ge(split_hi, 4 * i + 2 * n + k + 1)
                    dve.tensor_tensor(wl[s][:, a:b], raw[s][:, a:b], wh[s][:, a:b], ALU.subtract).then_inc(split_lo, 1)

            def gx(c, g, k):
                dve.wait_ge(gx_hi, k + c + 1)
                dve.scalar_tensor_tensor(out=gxl[:, c, :], in0=x[:, c, :], scalar=col(g + c), in1=gxh[:, c, :],
                                         op0=ALU.mult, op1=ALU.subtract).then_inc(gx_lo, 1)

            def out_bank(h, o):
                return bank[2 * (h % 2) + o]

            def wait_out(n, h, o):
                dve.wait_ge(half_ready, h + 1) if o == 0 else dve.wait_ge(unit_used, n + 1)

            def gate_step(n, h, i=None):
                k = 0 if i is None else 2 * i
                g = h - H_F0 if h < H_OIN else h - H_F1 + 2 * HC
                c = (g % HC) + k
                dve.wait_ge(half_ready, k + h + 1)
                if g:
                    dve.wait_ge(hid_lo, k + g)
                dve.tensor_tensor(gate_s[:], out_bank(h, 0)[:, :], rstd[:], ALU.mult).then_inc(out_read, 1)
                dve.wait_ge(unit_used, k + n + 1)
                dve.tensor_tensor(up_s[:], out_bank(h, 1)[:, :], rstd[:], ALU.mult).then_inc(out_read, 1)
                dve.wait_ge(silu_done, k + g + 1)
                dve.wait_ge(out_read, 2 * k + 2 * h + 2)
                dve.tensor_tensor(gate_s[:], gate_s[:], up_s[:], ALU.mult).then_inc(prod_done, 1)
                dve.wait_ge(hid_hi, k + g + 1)
                if i is None:
                    hi, lo = hidh[:, c, :], hidl[:, c, :]
                else:
                    hi = hidh[:, bass.ds(c, 1), :].rearrange("p a t -> p (a t)")
                    lo = hidl[:, bass.ds(c, 1), :].rearrange("p a t -> p (a t)")
                dve.tensor_tensor(lo, gate_s[:], hi, ALU.subtract).then_inc(hid_lo, 1)

            def rotate(src, direct, swapped):
                dve.tensor_tensor(direct[:], src[:], cosT[:], ALU.mult)
                for g in range(4):
                    a, b = 32 * g, 32 * (g ^ 1)
                    ins = dve.tensor_tensor(swapped[b:b + 32, :], src[a:a + 32, :], sinT[a:a + 32, :], ALU.mult)
                return ins

            def down_step(n, m, g, k, i=None):
                e = 0 if i is None else 2 * i
                dve.wait_ge(unit_used, e + n + 1)
                b = bank[4 + n % 2][:, :]
                if i is None:
                    xm, cm, hi, lo = x[:, m, :], None if g is None else col(g + m), gxh[:, m, :], gxl[:, m, :]
                else:
                    mm = e + m
                    xm = x[:, bass.ds(mm, 1), :].rearrange("p a t -> p (a t)")
                    hi = gxh[:, bass.ds(mm, 1), :].rearrange("p a t -> p (a t)")
                    lo = gxl[:, bass.ds(mm, 1), :].rearrange("p a t -> p (a t)")
                    cm = None if g is None else cols[:, bass.ds(g + mm, 1)]
                dve.tensor_tensor(xm, xm, b, ALU.add).then_inc(x_done, 1)
                if g is not None:
                    dve.wait_ge(gx_hi, e + k + m + 1)
                    dve.scalar_tensor_tensor(out=lo, in0=xm, scalar=cm, in1=hi,
                                             op0=ALU.mult, op1=ALU.subtract).then_inc(gx_lo, 1)

            def ffn(base, hbase, layer, gain_next):
                for half in range(2):
                    n, h = base + half * HALF_UNITS, hbase + half * HC
                    if half == 0:
                        dve.wait_ge(norm_done, 2 * layer + 3)
                    gate_step(n, h)
                    split(n + 2)
                    with dve.Fori(0, 4) as i:
                        for j in range(2):
                            gate_step(n + 1 + j, h + 1 + j, i)
                            split(n + 3 + j, i)
                    for c in range(9, 11):
                        gate_step(n + c, h + c)
                        split(n + c + 2)
                    g = gain_next if half == 1 else None
                    k = (2 * layer + 2) * KC
                    n += HC
                    with dve.Fori(0, 3) as i:
                        for j in range(2):
                            down_step(n + j, j, g, k, i)
                            split(n + 2 + j, i)
                    for m in range(6, 8):
                        down_step(n + m, m, g, k)
                        if n + m + 2 < N_UNITS:
                            split(n + m + 2)

            dve.memset(pwr[:], 0.0).then_inc(vconst, 1)
            dve.memset(sm[:, S_ONE:S_ONE + 1], 1.0)
            dve.memset(sm[:, S_ONE + 1:S_ONE + 2], EPS)
            dve.memset(ones[:], 1.0)
            for g in range(2):
                dve.memset(half_rows[64 * g:64 * g + 64, g:g + 1], 1.0)
                dve.memset(half_rows[64 * (1 - g):64 * (1 - g) + 64, g:g + 1], 0.0)
            dve.memset(z[:, 0:2], 0.0)
            for c in range(KC):
                gx(c, C_MIX, 0)
                if c == 1:
                    split(0)
            split(1)
            dve.wait_ge(consts_landed, 16 * 8)
            link(dve.tensor_copy(ang[:], posi[:]))
            link(dve.tensor_scalar(ang[:], ang[:], col(C_INVF), None, ALU.mult))
            link(dve.tensor_scalar(turn[:], ang[:], 0.15915494309189535, 12582912.0, ALU.mult, ALU.add))
            link(dve.tensor_scalar(turn[:], turn[:], 12582912.0, None, ALU.subtract))
            for part in (6.28125, 0.001934051513671875, 1.2556659e-06):
                link(dve.scalar_tensor_tensor(out=ang[:], in0=turn[:], scalar=-part, in1=ang[:],
                                              op0=ALU.mult, op1=ALU.add))
            dve.tensor_scalar(ang[:], ang[:], 3.1415925, -3.1415925, ALU.min, ALU.max).then_inc(vconst, 1)
            dve.wait_ge(aconst, 1)
            dve.tensor_tensor(wsl[:], wsr[:], wsh[:], ALU.subtract).then_inc(v_lo, 1)
            dve.wait_ge(aconst, 2)
            link(dve.tensor_tensor(hsin[:], hsin[:], hsin[:], ALU.mult))
            dve.tensor_scalar(cosT[:], hsin[:], -2.0, 1.0, ALU.mult, ALU.add)
            for g in range(3):
                dve.tensor_scalar(sinT[32 * g:32 * g + 32, :], turn[32 * g:32 * g + 32, :], -1.0 if g % 2 else 1.0,
                                  None, ALU.mult)
            dve.tensor_scalar(sinT[96:P, :], turn[96:P, :], -1.0, None, ALU.mult).then_inc(vconst, 1)

            split(2)
            dve.wait_ge(v_gelu, TT)
            split(3)
            g4 = gv[:].rearrange("p t (h d) -> p (t h) d", d=P)
            s16 = lambda a: sm[:, a:a + 16].rearrange("p (g e) -> p g e", e=1).broadcast_to([P, 16, P])
            link(dve.tensor_reduce(sm[:, S_SUM:S_SUM + 16], g4, AX.X, ALU.add))
            link(dve.tensor_scalar(sm[:, S_MEAN:S_MEAN + 16], sm[:, S_SUM:S_SUM + 16], 1.0 / P, None, ALU.mult))
            link(dve.tensor_tensor(g4, g4, s16(S_MEAN), ALU.subtract))
            link(dve.tensor_tensor(mixed[:], gv[:], gv[:], ALU.mult))
            link(dve.tensor_reduce(sm[:, S_SUM:S_SUM + 16], mixed[:].rearrange("p t (h d) -> p (t h) d", d=P),
                                   AX.X, ALU.add))
            dve.tensor_scalar(sm[:, S_VAR:S_VAR + 16], sm[:, S_SUM:S_SUM + 16], 1.0 / P, None,
                              ALU.mult).then_inc(v_stat, 1)
            dve.wait_ge(v_rs, 1)
            link(dve.tensor_tensor(g4, g4, s16(S_VR), ALU.mult))
            dve.tensor_tensor(gv[:], gv[:], lng[:].rearrange("p (a t) -> p a t", a=1).broadcast_to([P, TT, T]),
                              ALU.mult).then_inc(v_norm, 1)
            dve.wait_ge(v_hi, 1)
            dve.tensor_tensor(vnl[:], gv[:], vnh[:], ALU.subtract).then_inc(v_lo, 1)
            dve.wait_ge(norm_done, 1)
            nb = 0
            for k in range(2, 8):
                split(k + 2)
                for o in range(2):
                    q = 2 * (k - 2) + o
                    kind, j = EVEN_ORDER[q]
                    h = H_EIN + k - 2
                    wait_out(k, h, o)
                    src = out_bank(h, o)[:, :]
                    if kind == "c":
                        dve.tensor_tensor(cb[:], src, rstd[:], ALU.mult).then_inc(out_read, 1)
                    elif kind == "h":
                        dve.tensor_tensor(gate_s[:], src, rstd[:], ALU.mult).then_inc(out_read, 1)
                        dve.wait_ge(out_read, 2 * h + o + 1)
                        link(dve.tensor_tensor(z[:, 2:], gate_s[:], cb[:], ALU.mult))
                        taps = [cols[:, C_CONV + 3 * j + i:C_CONV + 3 * j + i + 1] for i in range(3)]
                        link(dve.tensor_scalar(y[:], z[:, 2:], taps[2], None, ALU.mult))
                        for i in (1, 0):
                            link(dve.scalar_tensor_tensor(out=y[:], in0=z[:, i:i + T], scalar=taps[i], in1=y[:],
                                                          op0=ALU.mult, op1=ALU.add))
                    else:
                        nb += 1
                        dve.tensor_tensor(gate_s[:], src, rstd[:], ALU.mult).then_inc(out_read, 1)
                        dve.wait_ge(out_read, 2 * h + o + 1)
                        dve.tensor_tensor(up_s[:], gate_s[:], y[:], ALU.mult).then_inc(mx_f, 1)
                        dve.wait_ge(mx_hi, nb)
                        dve.tensor_tensor(mixl[:, 4 + j, :], up_s[:], mixh[:, 4 + j, :],
                                          ALU.subtract).then_inc(mx_lo, 1)
            for h in range(4):
                dve.wait_ge(mix_mm, h + 1)
                dve.tensor_tensor(mixed[:, h, :].rearrange("p (n t) -> p n t", t=P),
                                  bank[4 + h][:, :].rearrange("p (n t) -> p n t", t=P),
                                  bbc[:, h:h + 1, :].broadcast_to([P, 4, P]), ALU.add).then_inc(mix_read, 1)
            for k in range(8, 10):
                for o in range(2):
                    j = 2 * (k - 8) + o
                    h = H_EIN + k - 2
                    wait_out(k, h, o)
                    dve.tensor_tensor(gate_s[:], out_bank(h, o)[:, :], rstd[:], ALU.mult).then_inc(out_read, 1)
                    dve.wait_ge(u_gelu, j + 1)
                    dve.wait_ge(mix_read, 4)
                    dve.tensor_tensor(up_s[:], gate_s[:], mixed[:, j, :], ALU.mult).then_inc(mx_f, 1)
                    dve.wait_ge(mx_hi, 5 + j)
                    dve.tensor_tensor(mixl[:, j, :], up_s[:], mixh[:, j, :], ALU.subtract).then_inc(mx_lo, 1)
                split(k + 2)

            def out_proj(base, hbase, g, k0):
                for k in range(4):
                    for o in range(2):
                        m = 2 * k + o
                        wait_out(base + k, hbase + k, o)
                        dve.tensor_tensor(x[:, m, :], x[:, m, :], out_bank(hbase + k, o)[:, :],
                                          ALU.add).then_inc(out_read, 1)
                        gx(m, g, k0)
                    split(base + k + 2)

            out_proj(U_EOUT, H_EOUT, C_FFN, KC)
            ffn(U_F0, H_F0, 0, C_MIX + KC)

            dve.wait_ge(norm_done, 4)
            for c in range(2):
                dve.memset(zp[c][:, 0:15], 0.0)
            for k in range(4):
                for o in range(2):
                    i = 2 * k + o
                    h = H_OIN + k
                    wait_out(U_OIN + k, h, o)
                    dst = lat[:, i, :] if i < 6 else zp[i - 6][:, 15:]
                    dve.tensor_tensor(dst, out_bank(h, o)[:, :], rstd[:], ALU.mult).then_inc(out_read, 1)
                    if i < 5:
                        dve.wait_ge(lat_hi, i + 1)
                        dve.scalar_tensor_tensor(out=latl[:, i, :], in0=lat[:, i, :], scalar=col(C_LAT + i),
                                                 in1=lath[:, i, :], op0=ALU.mult,
                                                 op1=ALU.subtract).then_inc(lat_lo, 1)
                split(U_OIN + k + 2)
            dve.wait_ge(lat_r, 1)
            link(dve.tensor_tensor(sm[:, S_RQ2:S_RQ2 + 4], sm[:, S_LAT:S_LAT + 4], sm[:, S_LAT:S_LAT + 4], ALU.mult))
            link(dve.tensor_scalar(rk[:], lat[:, 5, :], col(C_KGR), None, ALU.mult))
            link(rotate(rk, prob[0], prob[1]))
            dve.tensor_tensor(rk[:], prob[0][:], prob[1][:], ALU.add).then_inc(rk_done, 1)
            dve.wait_ge(aconst, 3)
            dve.tensor_tensor(pwl[:], pwr[:], pwh[:], ALU.subtract).then_inc(pw_lo, 1)

            for p in range(PAIRS):
                b = 10 * p
                if p == 0:
                    dve.wait_ge(lat_sq, 1)
                for o in range(2):
                    dve.wait_ge(proj_hi, 7 * p + o + 1)
                    dve.scalar_tensor_tensor(out=qnl[:, o, :], in0=bank[(b + o) % 3][:, :], scalar=col(C_QG),
                                             in1=qnh[:, o, :], op0=ALU.mult,
                                             op1=ALU.subtract).then_inc(proj_read, 1)
                dve.wait_ge(proj_sq, 5 * p + 3)
                dve.tensor_scalar(qx[:], bank[(b + 2) % 3][:, :], col(C_QGR), None, ALU.mult).then_inc(proj_read, 1)
                dve.wait_ge(proj, b + 4)
                rq = sm[:, S_RQ2:S_RQ2 + 4].rearrange("p (a t) -> p a t", a=1).broadcast_to([P, 2, 4])
                sq8 = sm[:, S_Q:S_Q + 8].rearrange("p (a t) -> p a t", a=2)
                dve.tensor_tensor(sq8, bank[(b + 3) % 3][:, 0:8].rearrange("p (a t) -> p a t", a=2), rq,
                                  ALU.mult).then_inc(proj_read, 1)
                dve.wait_ge(lat_r, 2)
                for o in range(2):
                    dve.wait_ge(proj, b + 5 + o)
                    dve.tensor_tensor(kk[:, o, :], bank[(b + 4 + o) % 3][:, :], rkv[:],
                                      ALU.mult).then_inc(proj_read, 1)
                dve.wait_ge(proj_read, 8 * p + 3)
                link(rotate(qx, qrot, krp))
                dve.tensor_tensor(qx[:], qrot[:], krp[:], ALU.add).then_inc(q_rot, 1)
                for o in range(2):
                    dve.wait_ge(proj_hi, 7 * p + 5 + 2 * o)
                    for t in range(2):
                        tt = 2 * o + t
                        ins = dve.scalar_tensor_tensor(out=vl[:, tt, :],
                                                       in0=bank[(b + 6 + o) % 3][:, t * 256:t * 256 + 256],
                                                       scalar=sm[:, S_LAT + 4 + tt:S_LAT + 5 + tt],
                                                       in1=vh[:, tt, :], op0=ALU.mult, op1=ALU.subtract)
                    ins.then_inc(proj_read, 1)
                dve.wait_ge(q_r, p + 1)
                lq = sm[:, S_LAT:S_LAT + 4].rearrange("p (a t) -> p a t", a=1).broadcast_to([P, 2, 4])
                dve.scalar_tensor_tensor(out=sm[:, S_SF:S_SF + 8].rearrange("p (a t) -> p a t", a=2), in0=sq8,
                                         scalar=SM_SCALE, in1=lq, op0=ALU.mult, op1=ALU.mult).then_inc(sf_done, 1)
                dve.wait_ge(q_rot, p + 1)
                dve.tensor_tensor(qrl[:], qx[:], qrh[:], ALU.subtract).then_inc(pair_lo, 1)
                for o in range(2):
                    dve.wait_ge(k_r, 2 * p + o + 1)
                    dve.scalar_tensor_tensor(out=kk[:, o, :], in0=kk[:, o, :], scalar=col(C_KG), in1=fk[:, o, :],
                                             op0=ALU.mult, op1=ALU.mult).then_inc(k_f, 1)
                dve.tensor_tensor(krp[0:64, :], rk[0:64, :], fk[0:64, 0, :], ALU.mult)
                dve.tensor_tensor(krp[64:P, :], rk[64:P, :], fk[64:P, 1, :], ALU.mult).then_inc(k_f, 1)
                for o in range(2):
                    dve.wait_ge(k_hi, 3 * p + o + 1)
                    dve.tensor_tensor(knl[:, o, :], kk[:, o, :], knh[:, o, :], ALU.subtract).then_inc(pair_lo, 1)
                dve.wait_ge(k_hi, 3 * p + 3)
                dve.tensor_tensor(krl[:], krp[:], krh[:], ALU.subtract).then_inc(pair_lo, 1)
                split(U_PAIR + p + 2)
                if p == 0:
                    for c in range(2):
                        dve.wait_ge(pooled_hi, c + 1)
                        dve.tensor_tensor(mixl[:, 2 + c, :], pm[c][:], mixh[:, 2 + c, :],
                                          ALU.subtract).then_inc(pooled_lo, 1)
                    for c in range(2):
                        dve.wait_ge(mx_hi, KC + c + 1)
                        dve.scalar_tensor_tensor(out=mixl[:, c, :], in0=bank[5 + c][:, :], scalar=col(C_PSCALE + c),
                                                 in1=mixh[:, c, :], op0=ALU.mult,
                                                 op1=ALU.subtract).then_inc(mx_lo, 1)
                dve.wait_ge(sf_done, p + 1)
                exped = None
                for what, hd, i in ATTENTION:
                    head = 2 * p + hd
                    q = 4 * head + i
                    if exped is not None:
                        dve.wait_ge(prob_exp, exped + 1)
                        e = exped % 4
                        dve.reciprocal(sm[:, S_RI + e:S_RI + e + 1], sm[:, S_RS + e:S_RS + e + 1]).then_inc(row_recip, 1)
                    exped = q if what == "S" else None
                    if what == "S":
                        dve.wait_ge(score, q + 1)
                        link(dve.tensor_reduce(sm[:, S_MX + i:S_MX + i + 1], bank[3 + q % 2][:, 0:P * (i + 1)],
                                               AX.X, ALU.max))
                        dve.scalar_tensor_tensor(out=sm[:, S_NB + i:S_NB + i + 1], in0=sm[:, S_MX + i:S_MX + i + 1],
                                                 scalar=-1.0, in1=sm[:, S_SF + 4 * hd + i:S_SF + 4 * hd + i + 1],
                                                 op0=ALU.mult, op1=ALU.mult).then_inc(score_max, 1)
                    elif what == "T":
                        dve.wait_ge(pt_hi, q + 1)
                        dve.tensor_tensor(ptl[:, 0:i + 1, P * i:P * i + P],
                                          bank[5 + q % 2][:, 0:P * (i + 1)].rearrange("p (j q) -> p j q", q=P),
                                          pth[:, 0:i + 1, P * i:P * i + P], ALU.subtract).then_inc(pt_lo, 1)
                    else:
                        dve.wait_ge(mx_hi, KC + 2 + head + 1)
                        dve.tensor_tensor(mixl[:, 2 + head, :], bank[7][:, :], mixh[:, 2 + head, :],
                                          ALU.subtract).then_inc(mx_lo, 1)

            out_proj(U_OOUT, H_OOUT, C_FFN + KC, 3 * KC)
            ffn(U_F1, H_F1, 1, None)

        @block.tensor
        def _(pe):
            def mm3(dst, wa, wb, xa, xb, start, stop):
                pe.matmul(dst, wb, xa, start=start, stop=False)
                pe.matmul(dst, wa, xb, start=False, stop=False)
                return pe.matmul(dst, wa, xa, start=False, stop=stop)

            def arrived(n, i=None):
                if i is None:
                    pe.wait_ge(split_lo, 2 * (n + 1))
                else:
                    pe.wait_ge(split_lo, 4 * i + 2 * (n + 1))

            def two_out(n, h, xh_, xl_, order=range(KC), before=None, width=(P, P), free=True):
                arrived(n)
                if free and h >= 2:
                    pe.wait_ge(out_read, 2 * (h - 1))
                s = n % 2
                for o in range(2):
                    for k, kc in enumerate(order):
                        if before:
                            before(o, kc)
                        a = (o * KC + kc) * P
                        ins = mm3(bank[2 * (h % 2) + o][:, :], wh[s][:, a:a + P], wl[s][:, a:a + P],
                                  xh_[:, kc, :], xl_[:, kc, :], k == 0, k == KC - 1)
                    ins.then_inc(half_ready if o == 0 else unit_used, 1)

            def norm(k):
                pe.wait_ge(sumsq, k)
                pe.matmul(bank[6][:, :], ones[:], acc[:], start=True, stop=True).then_inc(norm_mm, 1)

            def gate_body(n, h, i=None):
                s = n % 2
                for o in range(2):
                    for kc in range(KC):
                        a = (o * KC + kc) * P
                        ins = mm3(bank[2 * (h % 2) + o][:, :], wh[s][:, a:a + P], wl[s][:, a:a + P],
                                  gxh[:, kc, :], gxl[:, kc, :], kc == 0, kc == KC - 1)
                    ins.then_inc(half_ready if o == 0 else unit_used, 1)

            def down_body(n, m, g, done, i=None):
                arrived(n, i)
                if i is not None:
                    pe.wait_ge(x_done, 2 * i + done + m - 1)
                elif done:
                    pe.wait_ge(x_done, done)
                s = n % 2
                for kc in range(HC):
                    if kc in (0, HC - 1):
                        pe.wait_ge(hid_lo, g + HC - (kc == 0))
                    ks = slice(kc * P, kc * P + P)
                    ins = mm3(bank[4 + s][:, :], wh[s][:, ks], wl[s][:, ks], hidh[:, kc, :], hidl[:, kc, :],
                              kc == 0, kc == HC - 1)
                ins.then_inc(unit_used, 1)

            def ffn(base, hbase, layer):
                for half in range(2):
                    n, h = base + half * HALF_UNITS, hbase + half * HC
                    if half == 0:
                        two_out(n, h, gxh, gxl,
                                before=lambda o, kc: pe.wait_ge(gx_lo, (2 * layer + 1) * KC + kc + 1) if o == 0 else None)
                        norm(2 * layer + 2)
                    else:
                        two_out(n, h, gxh, gxl)
                    with pe.Fori(0, (HC - 1) // 2) as i:
                        for j in range(2):
                            arrived(n + 1 + j, i)
                            pe.wait_ge(out_read, 4 * i + 2 * (h + j))
                            gate_body(n + 1 + j, h + 1 + j)
                    n += HC
                    g = (2 * layer + half) * HC
                    for m in range(2):
                        down_body(n + m, m, g, (2 * layer + half) * KC)
                    with pe.Fori(0, KC // 2 - 1) as i:
                        for j in range(2):
                            down_body(n + 2 + j, 2 + j, g, (2 * layer + half) * KC, i)

            for n in range(2):
                arrived(n)
                for k in range(4):
                    kc = 4 * n + k
                    pe.wait_ge(gx_lo, kc + 1)
                    for t in range(TT):
                        a, b = k * T, k * T + T
                        ts = slice(t * P, t * P + P)
                        ins = mm3(bank[t][:, :], gxh[:, kc, ts], gxl[:, kc, ts], wh[n][:, a:b], wl[n][:, a:b],
                                  kc == 0, kc == KC - 1)
                ins.then_inc(unit_used, 1)
            norm(1)
            for t in range(TT):
                ins = pe.matmul(bank[7][:, t:t + 1], acc[:, t * P:t * P + P], ones[:, 0:1], start=True, stop=True)
            ins.then_inc(norm_mm, 1)
            for k in range(2, 10):
                if k < 4:
                    pe.wait_ge(v_gelu, 2 * k - 2)
                two_out(k, H_EIN + k - 2, gxh, gxl)
                if k == 7:
                    pe.wait_ge(v_lo, 2)
                    for h in range(4):
                        for c in range(TT):
                            hs, cs = slice(h * P, h * P + P), slice(c * P, c * P + P)
                            ins = mm3(bank[4 + h][:, cs], vnh[:, c, hs], vnl[:, c, hs], wsh[:, h, :], wsl[:, h, :],
                                      True, True)
                        ins.then_inc(mix_mm, 1)
            conv_first = [4, 5, 6, 7, 0, 1, 2, 3]
            for k in range(4):
                two_out(U_EOUT + k, H_EOUT + k, mixh, mixl, conv_first,
                        before=(lambda o, kc: pe.wait_ge(mx_lo, kc - 3 if kc > 3 else kc + 5) if o == 0 else None)
                        if k == 0 else None)
            ffn(U_F0, H_F0, 0)

            for k in range(4):
                two_out(U_OIN + k, H_OIN + k, gxh, gxl,
                        before=(lambda o, kc: pe.wait_ge(gx_lo, 2 * KC + kc + 1) if o == 0 else None)
                        if k == 0 else None)
                if k == 0:
                    norm(3)
            pe.wait_ge(lat_sq, 1)
            pe.wait_ge(norm_done, 4)
            for a, src in ((0, acc), (4, acckv)):
                for t in range(TT):
                    pe.matmul(bank[6][:, a + t:a + t + 1], src[:, t * P:t * P + P], ones[:, 0:1],
                              start=True, stop=True)
            pe.matmul(bank[7][:, :], ones[:], acckv[:], start=True, stop=True).then_inc(lat_mm, 1)

            for p in range(PAIRS):
                b = 10 * p
                n = U_PAIR + p
                arrived(n)
                s = n % 2
                k_at = QC * 3 * P
                v_at = k_at + KVC * 2 * P

                def free(o):
                    g = b + o - 3
                    if g < 0:
                        pe.wait_ge(out_read, 2 * H_OOUT)
                    elif g % 10 >= 8:
                        pe.wait_ge(k_r, 2 * (g // 10) + g % 10 - 7)
                    else:
                        pe.wait_ge(proj_read, 8 * (g // 10) + g % 10 + 1)

                pe.wait_ge(lat_lo, 5)
                for o in range(3):
                    free(o)
                    for kc in range(QC):
                        a = (kc * 3 + o) * P
                        ins = mm3(bank[(b + o) % 3][:, :], wh[s][:, a:a + P], wl[s][:, a:a + P],
                                  lath[:, kc, :], latl[:, kc, :], kc == 0, kc == QC - 1)
                    ins.then_inc(proj, 1)
                free(3)
                pe.wait_ge(proj_sq, 5 * p + 3)
                for hd in range(2):
                    for t in range(TT):
                        dst = bank[(b + 3) % 3][:, 4 * hd + t:4 * hd + t + 1]
                        ts = slice(t * P, t * P + P)
                        pe.matmul(dst, sq[:, hd, ts], ones[:, 0:1], start=True, stop=False)
                        ins = pe.matmul(dst, sqr[:, ts], half_rows[:, hd:hd + 1], start=False, stop=True)
                ins.then_inc(proj, 1)
                for o in range(2):
                    free(4 + o)
                    for kc in range(KVC):
                        a = k_at + (kc * 2 + o) * P
                        ins = mm3(bank[(b + 4 + o) % 3][:, :], wh[s][:, a:a + P], wl[s][:, a:a + P],
                                  lath[:, QC + kc, :], latl[:, QC + kc, :], kc == 0, kc == KVC - 1)
                    ins.then_inc(proj, 1)
                for o in range(2):
                    free(6 + o)
                    for t in range(2):
                        ts = slice((2 * o + t) * P, (2 * o + t) * P + P)
                        for kc in range(KVC):
                            a = v_at + kc * 2 * P
                            ins = mm3(bank[(b + 6 + o) % 3][:, t * 256:t * 256 + 256],
                                      lath[:, QC + kc, ts], latl[:, QC + kc, ts],
                                      wh[s][:, a:a + 256], wl[s][:, a:a + 256], kc == 0, kc == KVC - 1)
                    ins.then_inc(proj, 1)
                for o in range(2):
                    free(8 + o)
                    pe.wait_ge(proj_sq, 5 * p + 4 + o)
                    dst = bank[(b + 8 + o) % 3][:, :]
                    ins = pe.matmul(dst, ones[:], sq[:, o, :], start=True, stop=False)
                    if o == 0:
                        ins.then_inc(unit_used, 1)
                    pe.matmul(dst, ones[0:64, :], krsq[0:64, :], start=False, stop=True).then_inc(proj, 1)
                if p == 0:
                    pe.wait_ge(pw_lo, 1)
                    pe.wait_ge(pooled_lo, 2)
                    pe.wait_ge(lat_r, 2)
                    for c in range(2):
                        mm3(bank[5 + c][:, :], pwh[:, c, :], pwl[:, c, :], mixh[:, 2 + c, :], mixl[:, 2 + c, :],
                            True, True).then_inc(pool_mm, 1)
                pe.wait_ge(pair_lo, 4 * (p + 1))
                pe.wait_ge(proj_read, 8 * (p + 1))
                for what, hd, i in ATTENTION:
                    head = 2 * p + hd
                    q = 4 * head + i
                    N = P * (i + 1)
                    ts = slice(i * P, i * P + P)
                    if what == "S":
                        if q >= 2:
                            pe.wait_ge(prob_exp, q - 1)
                        r = slice(64 * hd, 64 * hd + 64)
                        dst = bank[3 + q % 2]
                        mm3(dst[:, 0:N], qnh[:, hd, ts], qnl[:, hd, ts], knh[:, hd, 0:N], knl[:, hd, 0:N], True, False)
                        mm3(dst[:, 0:N], qrh[r, ts], qrl[r, ts], krh[r, 0:N], krl[r, 0:N], False, False)
                        pe.matmul(dst[:, N - P:N], identr[:], maskr[:], start=False, stop=True).then_inc(score, 1)
                    elif what == "T":
                        pe.wait_ge(prob_n, q + 1)
                        if q >= 2:
                            pe.wait_ge(pt_lo, q - 1)
                        elif q == 0:
                            pe.wait_ge(mx_lo, KC + 2)
                        for j in range(i + 1):
                            js = slice(j * P, j * P + P)
                            ins = pe.transpose(bank[5 + q % 2][:, js], prob[q % 3][:, js], ident[:])
                        ins.then_inc(prob_t, 1)
                    else:
                        pe.wait_ge(pt_lo, 4 * (head + 1))
                        if head:
                            pe.wait_ge(mx_lo, KC + 2 + head)
                        for j in range(TT):
                            hs = slice(hd * P, hd * P + P)
                            ins = mm3(bank[7][:, j * P:T], vh[:, j, hs], vl[:, j, hs], pth[:, j, j * P:T],
                                      ptl[:, j, j * P:T], j == 0, j == TT - 1)
                        ins.then_inc(pv, 1)
            for k in range(4):
                two_out(U_OOUT + k, H_OOUT + k, mixh, mixl,
                        before=(lambda o, kc: pe.wait_ge(mx_lo, KC + kc + 1) if o == 0 else None)
                        if k == 0 else None)
            ffn(U_F1, H_F1, 1)


def kernel(**inputs):
    import numpy as np
    import concourse.bacc as bacc
    from concourse.bass_utils import run_bass_kernel_spmd

    a = {k: np.asarray(v) for k, v in inputs.items()}

    def chunks(w):
        k, m = w.shape
        return w.reshape(k // P, P, m // P, P).transpose(2, 1, 0, 3).reshape(m // P, P, k)

    def pairs(c, order):
        return np.stack([np.concatenate([c[order[i]], c[order[i + 1]]], axis=1) for i in range(0, len(order), 2)])

    ein = a["even_w_in"][0]
    v_units = ein[:, 512:1024].reshape(2, 4, P, 512).transpose(0, 2, 1, 3).reshape(2, P, W_UNIT)
    c = chunks(ein)
    at = {"b": 8, "c": 12, "h": 16}
    w_ein = np.concatenate([v_units, pairs(c, [at[k] + j for k, j in EVEN_ORDER] + [0, 1, 2, 3])])
    w_eout = pairs(chunks(a["even_w_out"][0]), list(range(8)))
    oin = a["odd_w_in"][0]
    c = chunks(np.concatenate([oin, oin[:, -64:]], axis=1))
    w_oin = pairs(c, [2, 3, 4, 5, 6, 7, 0, 1])
    w_oout = pairs(chunks(a["odd_w_out"][0]), list(range(8)))
    qb = a["q_b"][0].reshape(QC, P, HEADS, QK)
    kvb = a["kv_b"][0].reshape(KVC, P, HEADS, 2 * P)
    w_pair = []
    for h in range(0, HEADS, 2):
        q = np.concatenate([qb[:, :, h, :P], qb[:, :, h + 1, :P], qb[:, :, h, P:], qb[:, :, h + 1, P:]], axis=2)
        k = np.concatenate([kvb[:, :, h, :P], kvb[:, :, h + 1, :P]], axis=2)
        v = np.concatenate([kvb[:, :, h, P:], kvb[:, :, h + 1, P:]], axis=2)
        w_pair.append(np.concatenate([t.transpose(1, 0, 2).reshape(P, -1) for t in (q, k, v)], axis=1))
    w_pair = np.stack(w_pair)
    w_gu = np.stack([np.concatenate([chunks(a["ffn_w_gate"][l]), chunks(a["ffn_w_up"][l])], axis=2) for l in range(2)])
    w_dn = np.stack([np.concatenate([chunks(a["ffn_w_down"][l][h * HC * P:(h + 1) * HC * P]) for h in range(2)])
                     for l in range(2)])

    def columns(v):
        return v.reshape(-1, P).T

    conv = a["sc_conv_w"][0].reshape(3, 4, P).transpose(2, 1, 0).reshape(P, 12)
    twice = lambda v: np.concatenate([v, v])[:, None]
    qg, kg = a["q_norm"][0], a["k_norm"][0]
    freq = (10000.0 ** (-np.arange(0, 64, 2) / 64.0)).astype(np.float32)
    window = np.array([[2, 4], [8, 16]])
    row_window = np.repeat(window, 64, axis=1).T
    fix = row_window[:, :, None] / np.minimum(np.arange(1, 17)[None, None], row_window[:, :, None])
    cols = np.concatenate([
        columns(a["mix_norm"].reshape(-1)), columns(a["ffn_norm"].reshape(-1)), conv, columns(a["pool_scale"][0]),
        columns(a["q_a_norm"][0]), columns(a["kv_a_norm"][0]), qg[:P, None], twice(qg[P:]), kg[:P, None],
        twice(kg[P:]), np.tile(freq, 4)[:, None], (1.0 / row_window).astype(np.float32),
        fix.reshape(P, 32).astype(np.float32)], axis=1)

    arrays = {
        "xT": a["x"][0].T.reshape(KC, P, T).transpose(1, 0, 2),
        "pos": a["positions"],
        "cols": cols,
        "sg_g": a["sg_ln_g"],
        "sg_b": a["sg_b_s"].reshape(1, T),
        "sg_w": a["sg_w_s"][0].transpose(2, 0, 1),
        "pool_w": a["pool_w"][0],
        "w_ein": w_ein, "w_eout": w_eout, "w_oin": w_oin, "w_pair": w_pair, "w_oout": w_oout,
        "w_gu": w_gu, "w_dn": w_dn,
    }
    nc = bacc.Bacc("TRN2", target_bir_lowering=False, num_devices=1)
    feeds, args = {}, []
    for name, v in arrays.items():
        v = np.ascontiguousarray(v)
        feeds[f"in_{name}"] = v
        args.append(nc.dram_tensor(f"in_{name}", v.shape, mybir.dt.from_np(v.dtype), kind="ExternalInput").ap())
    args.append(nc.dram_tensor("out_T", (P, KC, T), F32, kind="ExternalOutput").ap())
    trunk(nc, *args)
    r = run_bass_kernel_spmd(nc, [feeds], core_ids=[0])
    return np.ascontiguousarray(r.results[0]["out_T"].transpose(1, 0, 2).reshape(D, T).T)[None]
```

```python
from contextlib import ExitStack

import concourse.bass as bass
from concourse import mybir

F32 = mybir.dt.float32
F32R = mybir.dt.float32r
BF16 = mybir.dt.bfloat16
I32 = mybir.dt.int32
ACT = mybir.ActivationFunctionType
ALU = mybir.AluOpType
AX = mybir.AxisListType

P = 128
T = 512
TT = T // P
D = 1024
KC = D // P
EPS = 1e-6
NEG = -2.0 ** 100
FF = 2816
HC = FF // P // 2
HEADS = 6
PAIRS = HEADS // 2
QK = 192
QC, KVC = 3, 2
SM_SCALE = QK ** -0.5

U_EIN, U_EOUT, U_F0 = 0, 10, 14
U_OIN, U_PAIR, U_OOUT, U_F1 = 52, 56, 59, 63
N_UNITS = 101
HALF_UNITS = HC + KC

H_EIN, H_EOUT, H_F0, H_OIN, H_OOUT, H_F1 = 0, 8, 12, 34, 38, 42

WARM_UP = 11

W_UNIT = 2 * KC * P
W_DOWN = HC * P
W_LAST_IN = KC * 2 * P
W_PAIR = QC * 3 * P + KVC * 2 * P + KVC * 2 * P
SLOT = max(W_UNIT, W_PAIR)

C_MIX, C_FFN, C_CONV, C_PSCALE, C_LAT, C_QG, C_QGR, C_KG, C_KGR, C_INVF, C_POOLW, C_POOLFIX, N_COLS = (
    0, 16, 32, 44, 46, 51, 52, 53, 54, 55, 56, 58, 90)
S_RV, S_SUM, S_MEAN, S_VAR, S_VR, S_LAT, S_RQ2, S_Q, S_SF, S_MX, S_NB, S_RS, S_RI, S_EPS, S_TABLE, N_SMALL = (
    0, 4, 20, 36, 52, 68, 76, 80, 88, 96, 104, 112, 120, 128, 129, 132)


EVEN_ORDER = [("c", 0), ("h", 0), ("b", 0), ("c", 1), ("h", 1), ("b", 1),
              ("c", 2), ("h", 2), ("b", 2), ("c", 3), ("h", 3), ("b", 3)]
PROJ = ["q0", "k0", "k1", "q1", "qr", "s0", "s1", "qs", "v0", "v1"]
FIRST = [("P", o) for o in range(7)] + [("F", 0), ("P", 7), ("P", 8), ("P", 9), ("G", 0), ("Q", 0)]
SCORES = [("S", 0, 0), ("S", 0, 1), ("S", 0, 2), ("S", 0, 3), ("S", 1, 0), ("T", 0, 0), ("S", 1, 1),
          ("T", 0, 1), ("E", 1, 0), ("S", 1, 2), ("T", 0, 2), ("S", 1, 3), ("T", 0, 3)]
VALUES = [("P", 0), ("V", 0), ("T", 1, 0), ("W", 0), ("W", 1), ("P", 1), ("T", 1, 1), ("P", 2), ("T", 1, 2),
          ("P", 3), ("T", 1, 3), ("P", 4), ("P", 5), ("P", 6), ("F", 0), ("V", 1), ("P", 7), ("P", 8), ("P", 9),
          ("G", 0), ("Q", 0)]
LAST_VALUES = [("O", 0), ("V", 0), ("T", 1, 0), ("T", 1, 1), ("W", 0), ("W", 1), ("O", 1), ("T", 1, 2), ("T", 1, 3),
               ("O", 2), ("V", 1)]


def pair_steps():
    steps = [(w, a, 0, 0) for w, a in FIRST]
    for p in range(PAIRS):
        steps += [(w, a, i, p) for w, a, i in SCORES]
        for w, a, *i in VALUES if p < PAIRS - 1 else LAST_VALUES:
            steps.append((w, a, i[0] if i else 0, p + (w in "PFGQ")))
    return steps


def maxima_first(steps):
    order, held = [], []
    for step in steps:
        if step[0] in "TE":
            held.append(step)
        elif step[0] == "S":
            order, held = order + [step] + held, []
        else:
            order, held = order + held + [step], []
    return order + held


def unit_width(n):
    for base in (U_F0, U_F1):
        if base <= n < base + 2 * HALF_UNITS:
            return W_UNIT if (n - base) % HALF_UNITS < HC else W_DOWN
    if U_PAIR <= n < U_OOUT:
        return W_PAIR
    return W_UNIT


def trunk(nc, xT, pos, cols_d, sg_g, sg_b, sg_w, pool_w, w_ein, w_eout, w_oin, w_pair, w_oout, w_gu, w_dn, out):
    with ExitStack() as ctx:
        def sem(name):
            return ctx.enter_context(nc.semaphore(name))

        here = [nc.sbuf_base + 31 & ~31]

        def at(name, shape, dt, offset):
            return nc.alloc_sbuf_tensor_at(name, shape, dt, offset=offset)

        def sb(name, shape, dt=F32):
            n = 4
            for s in shape[1:]:
                n *= s
            off = here[0]
            here[0] += n + 31 & ~31
            return at(name, shape, dt, off), off

        x, _ = sb("x", [P, KC, T])
        gxh, gx_at = sb("gxh", [P, KC, T], F32R)
        gxl, _ = sb("gxl", [P, KC, T], F32R)
        hidh, hidh_at = sb("hidh", [P, HC, T], F32R)
        hidl, hidl_at = sb("hidl", [P, HC, T], F32R)
        mixh, mixl = hidh, hidl
        raw = [sb(f"raw{i}", [P, SLOT])[0] for i in range(2)]
        wh = [sb(f"wh{i}", [P, SLOT], F32R)[0] for i in range(2)]
        wl = [sb(f"wl{i}", [P, SLOT], F32R)[0] for i in range(2)]
        rstd, _ = sb("rstd", [P, T])
        acc, _ = sb("acc", [P, T])
        gate_s, gate_at = sb("gate_s", [P, T])
        up_s, up_at = sb("up_s", [P, T])
        cosT, _ = sb("cosT", [P, T])
        sinT, _ = sb("sinT", [P, T])
        ident, _ = sb("ident", [P, P])
        identb, _ = sb("identb", [P, P], BF16)
        mask, _ = sb("mask", [P, P])
        maskb, _ = sb("maskb", [P, P], BF16)
        ones, _ = sb("ones", [P, P])
        half_rows, _ = sb("half_rows", [P, 2])
        head_ones, _ = sb("head_ones", [P, 2, 2])
        cols, _ = sb("cols", [P, N_COLS])
        sm, _ = sb("sm", [P, N_SMALL])
        pwr, _ = sb("pwr", [P, 2, P])
        mixer_at = here[0]

        gv, gv_at = sb("gv", [P, TT, T])
        vnh, _ = sb("vnh", [P, TT, T], F32R)
        vnl, _ = sb("vnl", [P, TT, T], F32R)
        mixed, _ = sb("mixed", [P, 4, T])
        wsr, _ = sb("wsr", [P, 4, P])
        wsh, _ = sb("wsh", [P, 4, P], F32R)
        wsl, _ = sb("wsl", [P, 4, P], F32R)
        bbc, _ = sb("bbc", [P, 4, P])
        lng, _ = sb("lng", [P, T])
        cb, _ = sb("cb", [P, T])
        z, _ = sb("z", [P, T + 2])
        y, _ = sb("y", [P, T])
        assert here[0] <= nc.sbuf_usable_end, here[0]

        posi = at("posi", [P, T], I32, gv_at)
        ang = at("ang", [P, T], F32, gv_at + 4 * T)
        turn = at("turn", [P, T], F32, gv_at + 8 * T)
        hsin = at("hsin", [P, T], F32, gv_at + 12 * T)

        here[0] = mixer_at
        lat, lat_at = sb("lat", [P, 6, T])
        lath, _ = sb("lath", [P, 5, T], F32R)
        latl, _ = sb("latl", [P, 5, T], F32R)
        rk = acc
        rkg = gate_s
        ptm, pt_at = sb("ptm", [P, 2 * TT * T])
        assert here[0] <= nc.sbuf_usable_end, here[0]
        pth = at("pth", [P, TT, T], F32R, pt_at)
        ptl = at("ptl", [P, TT, T], F32R, pt_at + 4 * TT * T)
        PADW = T + 15
        zp = [at(f"zp{c}", [P, PADW], F32, pt_at + c * 2112) for c in range(2)]
        win = [at(f"win{c}", [P, PADW], F32, pt_at + 4224 + c * 2112) for c in range(2)]
        pm = [at(f"pm{c}", [P, T], F32, pt_at + 8448 + c * 4 * T) for c in range(2)]

        def tile_of(i):
            return slice(P * i * (i + 1) // 2, P * (i + 1) * (i + 2) // 2)

        pwh = at("pwh", [P, 2, P], F32R, pt_at + 12544)
        pwl = at("pwl", [P, 2, P], F32R, pt_at + 13568)
        sqk = at("sqk", [P, 2, T], F32, lat_at)
        sqq = at("sqq", [P, 2, T], F32, lat_at + 8 * T)
        sqr = at("sqr", [P, T], F32, lat_at + 16 * T)
        qx = at("qx", [P, T], F32, lat_at + 20 * T)
        krp = at("krp", [P, T], F32, lat_at)
        fk = at("fk", [P, 2, T], F32, gate_at)
        assert up_at == gate_at + 4 * T
        PROBW = P * TT * (TT + 1) // 2
        prob = [at("prob0", [P, PROBW], F32, lat_at), at("prob1", [P, PROBW], F32, hidh_at + 8 * 4 * T)]
        rot = [at(f"rot{i}", [P, T], F32, hidh_at + (8 + i) * 4 * T) for i in range(2)]
        qdir, qswap = rot
        acckv = at("acckv", [P, T], F32, hidh_at + 10 * 4 * T)
        rkv = rstd
        kk = at("kk", [P, 2, T], F32, hidl_at + 8 * 4 * T)
        krsq = at("krsq", [P, T], F32, hidl_at + 10 * 4 * T)
        G = gx_at
        qnh = at("qnh", [P, 2, T], F32R, G)
        qnl = at("qnl", [P, 2, T], F32R, G + 8 * T)
        knh = at("knh", [P, 2, T], F32R, G + 16 * T)
        knl = at("knl", [P, 2, T], F32R, G + 24 * T)
        qrh = at("qrh", [P, T], F32R, G + 32 * T)
        qrl = at("qrl", [P, T], F32R, G + 36 * T)
        krh = at("krh", [P, T], F32R, G + 40 * T)
        krl = at("krl", [P, T], F32R, G + 44 * T)
        vh = at("vh", [P, TT, 2 * P], F32R, G + 48 * T)
        vl = at("vl", [P, TT, 2 * P], F32R, G + 56 * T)

        bank = [ctx.enter_context(nc.psum_tensor(f"bank{i}", [P, T], F32)) for i in range(8)]

        w0_landed = [sem(f"w0_landed{k}") for k in range(3)]
        w1_landed = sem("w1_landed")
        x_landed = [sem(f"x_landed{c}") for c in range(KC)]
        cols_landed = sem("cols_landed")
        consts_landed = sem("consts_landed")
        raw_landed = [sem("raw_landed0"), sem("raw_landed1")]
        first_hi = sem("first_hi")
        first_lo = sem("first_lo")
        split_hi = sem("split_hi")
        split_lo = sem("split_lo")
        half_ready = sem("half_ready")
        unit_used = sem("unit_used")
        out_read = sem("out_read")
        x_done = sem("x_done")
        gx_hi = sem("gx_hi")
        gx_lo = sem("gx_lo")
        sumsq = sem("sumsq")
        norm_mm = sem("norm_mm")
        norm_done = sem("norm_done")
        silu_done = sem("silu_done")
        prod_done = sem("prod_done")
        hid_hi = sem("hid_hi")
        hid_lo = sem("hid_lo")
        pool_ready = sem("pool_ready")
        pool_chain = sem("pool_chain")
        dve_chain = sem("dve_chain")
        act_chain = sem("act_chain")
        vconst = sem("vconst")
        aconst = sem("aconst")
        v_gelu = sem("v_gelu")
        v_mean = sem("v_mean")
        v_sq = sem("v_sq")
        v_stat = sem("v_stat")
        v_rs = sem("v_rs")
        v_norm = sem("v_norm")
        v_hi = sem("v_hi")
        v_lo = sem("v_lo")
        mix_mm = sem("mix_mm")
        mix_read = sem("mix_read")
        mx_f = sem("mx_f")
        mx_hi = sem("mx_hi")
        mx_lo = sem("mx_lo")
        u_gelu = sem("u_gelu")
        lat_hi = sem("lat_hi")
        lat_lo = sem("lat_lo")
        lat_sq = sem("lat_sq")
        lat_mm = sem("lat_mm")
        lat_r = sem("lat_r")
        rk_done = sem("rk_done")
        pooled = sem("pooled")
        pooled_hi = sem("pooled_hi")
        pooled_lo = sem("pooled_lo")
        pw_lo = sem("pw_lo")
        pool_mm = sem("pool_mm")
        sf_done = sem("sf_done")
        proj = sem("proj")
        proj_read = sem("proj_read")
        proj_sq = sem("proj_sq")
        proj_hi = sem("proj_hi")
        q_rot = sem("q_rot")
        pair_lo = sem("pair_lo")
        k_ln = sem("k_ln")
        k_sum = sem("k_sum")
        kr_f = sem("kr_f")
        kr_v = sem("kr_v")
        q_dir = sem("q_dir")
        k_r = sem("k_r")
        k_f = sem("k_f")
        k_hi = sem("k_hi")
        q_r = sem("q_r")
        score = sem("score")
        score_max = sem("score_max")
        prob_exp = sem("prob_exp")
        row_recip = sem("row_recip")
        prob_n = sem("prob_n")
        prob_t = sem("prob_t")
        pt_hi = sem("pt_hi")
        pt_lo = sem("pt_lo")
        pv = sem("pv")
        stored = sem("stored")

        block = ctx.enter_context(nc.Block())

        def col(c):
            return cols[:, c:c + 1]

        g4 = gv[:].rearrange("p t (h d) -> p (t h) d", d=P)

        def s16(a):
            return sm[:, a:a + 16].rearrange("p (g e) -> p g e", e=1).broadcast_to([P, 16, P])

        def s_bank(q):
            return bank[(3, 4, 7, (10 * (q // 8) + 7) % 3, 3, 4, 7, 3)[q % 8]]

        @block.sync
        def _(sp):
            def load(n, src, width):
                if n >= 2:
                    sp.wait_ge(split_lo, 2 * (n - 1))
                sp.dma_start(raw[n % 2][:, 0:width], src).then_inc(raw_landed[n % 2], 16)

            def load_loop(n0, count, src, width):
                assert count % 2 == 0
                with sp.Fori(0, count // 2) as i:
                    for j in range(2):
                        sp.wait_ge(split_lo, 4 * i + 2 * (n0 + j - 1))
                        sp.dma_start(raw[(n0 + j) % 2][:, 0:width],
                                     src(2 * i + j)).then_inc(raw_landed[(n0 + j) % 2], 16)

            def ffn(layer, base):
                for half in range(2):
                    n = base + half * HALF_UNITS
                    load(n, w_gu[layer, half * HC], W_UNIT)
                    load_loop(n + 1, HC - 1,
                              lambda i: w_gu[layer, bass.ds(half * HC + 1 + i, 1)].rearrange("a p w -> p (a w)"),
                              W_UNIT)
                    load_loop(n + HC, KC,
                              lambda i: w_dn[layer, bass.ds(half * KC + i, 1)].rearrange("a p w -> p (a w)"), W_DOWN)

            sp.dma_start(cols[:], cols_d).then_inc(cols_landed, 16)
            sp.dma_start(x[:, 0, :], xT[:, 0, :]).then_inc(x_landed[0], 16)
            for k in range(4):
                sp.dma_start(raw[0][:, k * T:k * T + T],
                             w_ein[0][:, k * T:k * T + T]).then_inc(w0_landed[k] if k < 3 else raw_landed[0], 16)
                if k < 3:
                    sp.dma_start(x[:, k + 1, :], xT[:, k + 1, :]).then_inc(x_landed[k + 1], 16)
            for c in range(4, KC):
                sp.dma_start(x[:, c, :], xT[:, c, :]).then_inc(x_landed[c], 16)
            half = W_UNIT // 2
            sp.dma_start(raw[1][:, 0:half], w_ein[1][:, 0:half]).then_inc(w1_landed, 16)
            sp.dma_start(raw[1][:, half:W_UNIT], w_ein[1][:, half:]).then_inc(raw_landed[1], 16)
            sp.wait_ge(vconst, 1)
            for c in range(2):
                for g in range(2):
                    sp.dma_start(pwr[64 * g:64 * g + 64, c, 64 * g:64 * g + 64],
                                  pool_w[2 * c + g]).then_inc(consts_landed, 16)
            sp.dma_start(posi[:], pos.broadcast_to([P, T])).then_inc(consts_landed, 16)
            sp.dma_start(wsr[:], sg_w).then_inc(consts_landed, 16)
            sp.dma_start(bbc[:].rearrange("p a b -> p (a b)"), sg_b.broadcast_to([P, T])).then_inc(consts_landed, 16)
            sp.dma_start(lng[:], sg_g.broadcast_to([P, T])).then_inc(consts_landed, 16)
            for k in range(2, 10):
                load(U_EIN + k, w_ein[k], W_UNIT)
            for k in range(4):
                load(U_EOUT + k, w_eout[k], W_UNIT)
            ffn(0, U_F0)
            for k in range(4):
                load(U_OIN + k, w_oin[k], W_UNIT)
            for k in range(PAIRS):
                load(U_PAIR + k, w_pair[k], W_PAIR)
            for k in range(4):
                load(U_OOUT + k, w_oout[k], W_UNIT)
            ffn(1, U_F1)
            for m in range(KC):
                sp.wait_ge(x_done, 3 * KC + m + 1)
                sp.dma_start(out[:, m, :], x[:, m, :]).then_inc(stored, 16)
            sp.wait_ge(stored, 16 * KC)

        @block.gpsimd
        def _(pool):
            links = [0]

            def link(ins):
                links[0] += 1
                ins.then_inc(pool_chain, 1)
                pool.wait_ge(pool_chain, links[0])

            link(pool.memset(ident[:], 0.0))
            pool.affine_select(out=ident[:], in_=ident[:], compare_op=ALU.not_equal, fill=1.0, base=0,
                               pattern=[[-1, P]], channel_multiplier=1).then_inc(pool_ready, 1)
            link(pool.memset(mask[:], 0.0))
            pool.affine_select(out=mask[:], in_=mask[:], compare_op=ALU.is_ge, fill=NEG, base=0,
                               pattern=[[-1, P]], channel_multiplier=1).then_inc(pool_ready, 1)
            def residual_sumsq(ready, sqx):
                for c in range(KC):
                    ready(c)
                    if c == 0:
                        link(pool.tensor_tensor(acc[:], x[:, c, :], x[:, c, :], ALU.mult))
                    else:
                        link(pool.tensor_tensor(sqx, x[:, c, :], x[:, c, :], ALU.mult))
                        ins = pool.tensor_tensor(acc[:], acc[:], sqx, ALU.add)
                        if c < KC - 1:
                            link(ins)
                        else:
                            ins.then_inc(sumsq, 1)

            residual_sumsq(lambda c: pool.wait_ge(x_landed[c], 16), y[:])
            pool.wait_ge(consts_landed, 16 * 8)
            pool.affine_select(out=wsr[:], in_=wsr[:], compare_op=ALU.is_ge, fill=0.0, base=0,
                               pattern=[[0, 4], [1, P]], channel_multiplier=-1).then_inc(pool_ready, 1)
            pool.wait_ge(v_mean, 1)
            pool.wait_ge(pool_ready, 3)
            link(pool.tensor_tensor(g4, g4, s16(S_MEAN), ALU.subtract))
            pool.tensor_tensor(mixed[:], gv[:], gv[:], ALU.mult).then_inc(v_sq, 1)
            pool.wait_ge(v_rs, 1)
            link(pool.tensor_tensor(g4, g4, s16(S_VR), ALU.mult))
            pool.tensor_tensor(gv[:], gv[:], lng[:].rearrange("p (a t) -> p a t", a=1).broadcast_to([P, TT, T]),
                               ALU.mult).then_inc(v_norm, 1)
            residual_sumsq(lambda c: pool.wait_ge(out_read, 2 * H_EOUT + c + 1), cb[:])
            residual_sumsq(lambda c: pool.wait_ge(x_done, KC + c + 1), cb[:])

            for c in range(2):
                pool.wait_ge(out_read, 2 * H_OIN + 1 + c)
                src, width = zp[c], 1
                for s in range(2 * c + 2):
                    dst = win[s % 2]
                    lo = 2 * width - 1
                    link(pool.tensor_tensor(dst[:, lo:], src[:, lo:], src[:, lo - width:PADW - width], ALU.add))
                    src, width = dst, 2 * width
                for r, w in ((slice(0, 64), win[0]), (slice(64, P), win[1])):
                    link(pool.tensor_scalar(pm[c][r, :], w[r, 15:], cols[r, C_POOLW + c:C_POOLW + c + 1], None,
                                            ALU.mult))
                link(pool.tensor_tensor(pm[c][:, 0:16], pm[c][:, 0:16],
                                        cols[:, C_POOLFIX + 16 * c:C_POOLFIX + 16 * c + 16], ALU.mult))
                ins = pool.tensor_tensor(pm[c][:], pm[c][:], zp[c][:, 15:], ALU.subtract)
                ins.then_inc(pooled, 1)
                pool.wait_ge(pooled, c + 1)

            pool.wait_ge(norm_mm, 4)
            for i in range(QC + KVC):
                pool.wait_ge(out_read, 2 * H_OIN + i + 3)
                total = acc if i < QC else acckv
                if i in (0, QC):
                    ins = pool.tensor_tensor(total[:], lat[:, i, :], lat[:, i, :], ALU.mult)
                else:
                    link(pool.tensor_tensor(krsq[:], lat[:, i, :], lat[:, i, :], ALU.mult))
                    ins = pool.tensor_tensor(total[:], total[:], krsq[:], ALU.add)
                if i < QC + KVC - 1:
                    link(ins)
                else:
                    ins.then_inc(lat_sq, 1)
                    pool.wait_ge(lat_sq, 1)
            pool.wait_ge(out_read, 2 * H_OIN + 8)
            link(pool.tensor_scalar(krsq[:], lat[:, 5, :], 0.5, None, ALU.mult))
            pool.tensor_tensor(krsq[:], krsq[:], lat[:, 5, :], ALU.mult).then_inc(lat_sq, 1)
            pool.wait_ge(lat_sq, 2)

            for what, a, i, p in pair_steps():
                kind = PROJ[a] if what == "P" else ""
                if kind in ("k0", "k1"):
                    pool.wait_ge(proj_sq, 5 * p + a + 1)
                    pool.tensor_tensor(sqk[:, a - 1, :], sqk[:, a - 1, :], krsq[:], ALU.add).then_inc(k_sum, 1)
                elif kind == "qr":
                    pool.wait_ge(k_sum, 2 * p + 2)
                    pool.wait_ge(proj_read, 8 * p + 5)
                    if p:
                        pool.wait_ge(prob_t, 8 * p)
                    pool.tensor_tensor(qdir[:], qx[:], cosT[:], ALU.mult).then_inc(q_dir, 1)
                elif what == "F":
                    pool.wait_ge(rk_done, 1)
                    pool.wait_ge(q_dir, p + 1)
                    pool.wait_ge(k_r, 2 * p + 1)
                    pool.tensor_tensor(krp[0:64, :], rk[0:64, :], fk[0:64, 0, :], ALU.mult).then_inc(kr_f, 1)
                elif what == "S":
                    q = 4 * (2 * p + a) + i
                    pool.wait_ge(row_recip, q + 1)
                    t = prob[a][:, tile_of(i)]
                    pool.tensor_scalar(t, t, sm[:, S_RI + q % 8:S_RI + q % 8 + 1], None, ALU.mult).then_inc(prob_n, 1)

            residual_sumsq(lambda c: pool.wait_ge(out_read, 2 * H_OOUT + c + 1), gate_s[:])

        @block.scalar
        def _(act):
            links = [0]

            def link(ins):
                links[0] += 1
                ins.then_inc(act_chain, 1)
                act.wait_ge(act_chain, links[0])

            def split(n, i=None, halves=(0, 1)):
                s = n % 2
                w = unit_width(n)
                if i is None:
                    act.wait_ge(raw_landed[s], 16 * (n // 2 + 1))
                    if n >= 2:
                        act.wait_ge(unit_used, n - 1)
                else:
                    act.wait_ge(raw_landed[s], 16 * i + 16 * (n // 2 + 1))
                    act.wait_ge(unit_used, 2 * i + n - 1)
                for k in halves:
                    a, b = k * (w // 2), (k + 1) * (w // 2)
                    act.activation(wh[s][:, a:b], raw[s][:, a:b], ACT.Copy).then_inc(split_hi, 1)

            def rsqrt(dst, src, scale):
                link(act.activation(dst, src, ACT.Ln, bias=sm[:, S_EPS:S_EPS + 1], scale=scale))
                return act.activation(dst, dst, ACT.Exp, scale=-0.5)

            def norm(k):
                act.wait_ge(norm_mm, k)
                rsqrt(rstd[:], bank[6][:, :], 1.0 / D).then_inc(norm_done, 1)

            def gx(c, g):
                act.activation(gxh[:, c, :], x[:, c, :], ACT.Copy, scale=col(g + c)).then_inc(gx_hi, 1)

            def gate_step(n, h, i=None):
                k = 0 if i is None else 2 * i
                g = h - H_F0 if h < H_OIN else h - H_F1 + 2 * HC
                c = (g % HC) + k
                act.wait_ge(out_read, 2 * k + 2 * h + 1)
                act.activation(gate_s[:], gate_s[:], ACT.Silu).then_inc(silu_done, 1)
                act.wait_ge(prod_done, k + g + 1)
                dst = hidh[:, c, :] if i is None else hidh[:, bass.ds(c, 1), :].rearrange("p a t -> p (a t)")
                act.activation(dst, gate_s[:], ACT.Copy).then_inc(hid_hi, 1)

            def down_gx(g, k, m, i=None):
                if i is None:
                    act.wait_ge(x_done, k + m + 1)
                    gx(m, g)
                else:
                    act.wait_ge(x_done, 2 * i + k + m + 1)
                    mm = 2 * i + m
                    act.activation(gxh[:, bass.ds(mm, 1), :].rearrange("p a t -> p (a t)"),
                                   x[:, bass.ds(mm, 1), :].rearrange("p a t -> p (a t)"), ACT.Copy,
                                   scale=cols[:, bass.ds(g + mm, 1)]).then_inc(gx_hi, 1)

            def ffn(base, hbase, layer, gain_next):
                for half in range(2):
                    n, h = base + half * HALF_UNITS, hbase + half * HC
                    if half == 0:
                        norm(2 * layer + 3)
                    gate_step(n, h)
                    split(n + 2)
                    with act.Fori(0, 4) as i:
                        for j in range(2):
                            gate_step(n + 1 + j, h + 1 + j, i)
                            split(n + 3 + j, i)
                    for c in range(9, 11):
                        gate_step(n + c, h + c)
                        split(n + c + 2)
                    k = (2 * layer + half) * KC
                    n += HC
                    with act.Fori(0, 3) as i:
                        for j in range(2):
                            if half == 1 and gain_next is not None:
                                down_gx(gain_next, k, j, i)
                            split(n + 2 + j, i)
                    for m in range(6, 8):
                        if half == 1 and gain_next is not None:
                            down_gx(gain_next, k, m)
                        if n + m + 2 < N_UNITS:
                            split(n + m + 2)

            act.wait_ge(pool_ready, 2)
            act.activation(identb[:], ident[:], ACT.Copy)
            act.activation(maskb[:], mask[:], ACT.Copy)
            act.wait_ge(cols_landed, 16)
            for c in range(KC):
                act.wait_ge(x_landed[c], 16)
                gx(c, C_MIX)
                if c < 4:
                    act.wait_ge(w0_landed[c] if c < 3 else raw_landed[0], 16)
                    act.activation(wh[0][:, c * T:c * T + T], raw[0][:, c * T:c * T + T],
                                   ACT.Copy).then_inc(split_hi if c % 2 else first_hi, 1)
            act.wait_ge(w1_landed, 16)
            act.activation(wh[1][:, 0:W_UNIT // 2], raw[1][:, 0:W_UNIT // 2], ACT.Copy).then_inc(split_hi, 1)
            act.wait_ge(raw_landed[1], 16)
            act.activation(wh[1][:, W_UNIT // 2:W_UNIT], raw[1][:, W_UNIT // 2:W_UNIT],
                           ACT.Copy).then_inc(split_hi, 1)
            act.wait_ge(vconst, 2)
            act.activation(hsin[:], ang[:], ACT.Sin, scale=0.5)
            act.activation(turn[:], ang[:], ACT.Sin).then_inc(aconst, 1)
            split(2)
            act.wait_ge(pool_ready, 3)
            act.activation(wsh[:], wsr[:], ACT.Copy).then_inc(aconst, 1)

            act.wait_ge(norm_mm, 2)
            act.activation(rstd[:], bank[2][:, :], ACT.Ln, bias=sm[:, S_EPS:S_EPS + 1], scale=1.0 / D)
            link(act.activation(sm[:, S_RV:S_RV + TT], bank[3][:, 0:TT], ACT.Ln, bias=sm[:, S_EPS:S_EPS + 1],
                                scale=1.0 / D))
            act.activation(rstd[:], rstd[:], ACT.Exp, scale=-0.5).then_inc(norm_done, 1)
            act.activation(sm[:, S_RV:S_RV + TT], sm[:, S_RV:S_RV + TT], ACT.Exp, scale=-0.5).then_inc(norm_done, 1)
            split(3)
            act.wait_ge(norm_done, 2)
            act.wait_ge(vconst, 3)
            for t in range(TT):
                act.activation(gv[:, t, :], bank[4 + t][:, :], ACT.Gelu,
                               scale=sm[:, S_RV + t:S_RV + t + 1]).then_inc(v_gelu, 1)
            gates = 0
            for k in range(2, 8):
                split(k + 2)
                for kind, j in EVEN_ORDER[2 * (k - 2):2 * (k - 2) + 2]:
                    if kind == "b":
                        gates += 1
                        act.wait_ge(mx_f, gates)
                        act.activation(mixh[:, 4 + j, :], up_s[:], ACT.Copy).then_inc(mx_hi, 1)
                if k == 3:
                    act.wait_ge(v_stat, 1)
                    rsqrt(sm[:, S_VR:S_VR + 16], sm[:, S_VAR:S_VAR + 16], 1.0).then_inc(v_rs, 1)
                if k == 5:
                    act.wait_ge(v_norm, 1)
                    act.activation(vnh[:], gv[:], ACT.Copy).then_inc(v_hi, 1)
            for k in range(8, 10):
                for o in range(2):
                    j = 2 * (k - 8) + o
                    act.wait_ge(out_read, 2 * (H_EIN + k - 2) + o + 1)
                    act.activation(gate_s[:], gate_s[:], ACT.Gelu).then_inc(u_gelu, 1)
                    act.wait_ge(mx_f, 5 + j)
                    act.activation(mixh[:, j, :], up_s[:], ACT.Copy).then_inc(mx_hi, 1)
                split(k + 2)
            for k in range(4):
                for o in range(2):
                    act.wait_ge(out_read, 2 * (H_EOUT + k) + o + 1)
                    gx(2 * k + o, C_FFN)
                split(U_EOUT + k + 2)

            ffn(U_F0, H_F0, 0, C_MIX + KC)

            norm(4)
            act.activation(pwh[:], pwr[:], ACT.Copy).then_inc(aconst, 1)
            for k in range(4):
                for o in range(2):
                    i = 2 * k + o - 2
                    if 0 <= i < QC + KVC:
                        act.wait_ge(out_read, 2 * H_OIN + i + 3)
                        act.activation(lath[:, i, :], lat[:, i, :], ACT.Copy, scale=col(C_LAT + i)).then_inc(lat_hi, 1)
                split(U_OIN + k + 2)
                if k == 2:
                    for c in range(2):
                        act.wait_ge(pooled, c + 1)
                        act.activation(mixh[:, 2 + c, :], pm[c][:], ACT.Copy).then_inc(pooled_hi, 1)
            def latent_scales():
                act.wait_ge(lat_mm, 1)
                eps = sm[:, S_EPS:S_EPS + 1]
                act.activation(sm[:, S_LAT:S_LAT + 4], bank[6][:, 0:4], ACT.Ln, bias=eps, scale=1.0 / (QC * P))
                act.wait_ge(out_read, 2 * H_OIN + 8)
                act.activation(rkv[:], bank[7][:, :], ACT.Ln, bias=eps, scale=1.0 / (KVC * P))
                link(act.activation(sm[:, S_LAT + 4:S_LAT + 8], bank[6][:, 4:8], ACT.Ln, bias=eps,
                                    scale=1.0 / (KVC * P)))
                act.activation(rkv[:], rkv[:], ACT.Exp, scale=-0.5).then_inc(lat_r, 1)
                act.activation(sm[:, S_LAT:S_LAT + 8], sm[:, S_LAT:S_LAT + 8], ACT.Exp, scale=-0.5).then_inc(lat_r, 1)

            def values_out(p, a):
                act.wait_ge(proj, 9 * p + 9) if a == 0 else act.wait_ge(unit_used, U_PAIR + p + 1)
                for t in range(2):
                    tt = 2 * a + t
                    act.activation(vh[:, tt, :], bank[(10 * p + 8 + a) % 3][:, t * 256:t * 256 + 256], ACT.Copy,
                                   scale=sm[:, S_LAT + 4 + tt:S_LAT + 5 + tt]).then_inc(proj_hi, 1)

            for what, a, i, p in pair_steps():
                b = 10 * p
                head = 2 * p + a
                q = 4 * head + i
                src = bank[(b + a) % 3][:, :]
                kind = PROJ[a] if what == "P" else ""
                if kind in ("k0", "k1"):
                    if p == 0 and kind == "k0":
                        latent_scales()
                    act.wait_ge(proj_read, 8 * p + a + 1)
                    act.activation(sqk[:, a - 1, :], kk[:, a - 1, :], ACT.Square).then_inc(proj_sq, 1)
                elif kind in ("q0", "q1"):
                    o = a // 3
                    if p == 0 and o == 0:
                        act.wait_ge(lat_lo, QC + KVC)
                        act.wait_ge(lat_sq, 1)
                    act.wait_ge(proj, 9 * p + a + 1)
                    act.activation(sqq[:, o, :], src, ACT.Square).then_inc(proj_sq, 1)
                    act.activation(qnh[:, o, :], src, ACT.Copy, scale=col(C_QG)).then_inc(proj_hi, 1)
                elif kind == "qr":
                    act.wait_ge(proj, 9 * p + a + 1)
                    act.activation(sqr[:], src, ACT.Square).then_inc(proj_sq, 1)
                    if p == 0:
                        for c in range(2):
                            act.wait_ge(pool_mm, c + 1)
                            act.activation(mixh[:, c, :], bank[3 + c][:, :], ACT.Copy,
                                           scale=col(C_PSCALE + c)).then_inc(mx_hi, 1)
                elif what == "F":
                    for o in range(2):
                        act.wait_ge(proj, 9 * p + 6 + o)
                        act.activation(fk[:, o, :], bank[(b + 5 + o) % 3][:, :], ACT.Ln, bias=sm[:, S_EPS:S_EPS + 1],
                                       scale=1.0 / QK).then_inc(k_ln, 1)
                    act.wait_ge(k_ln, 2 * p + 2)
                    for o in range(2):
                        act.activation(fk[:, o, :], fk[:, o, :], ACT.Exp, scale=-0.5).then_inc(k_r, 1)
                elif what == "G":
                    act.wait_ge(k_f, 2 * p + 1)
                    act.activation(knh[:, 0, :], kk[:, 0, :], ACT.Copy).then_inc(k_hi, 1)
                    act.wait_ge(q_rot, p + 1)
                    act.activation(qrh[:], qx[:], ACT.Copy).then_inc(k_hi, 1)
                    act.wait_ge(kr_f, p + 1)
                    act.wait_ge(kr_v, p + 1)
                    act.activation(krh[:], krp[:], ACT.Copy).then_inc(k_hi, 1)
                    act.wait_ge(k_f, 2 * p + 2)
                    act.activation(knh[:, 1, :], kk[:, 1, :], ACT.Copy).then_inc(k_hi, 1)
                elif what == "Q":
                    sq = sm[:, S_Q:S_Q + 8]
                    act.activation(sm[:, S_TABLE:S_TABLE + 1], sm[:, S_EPS:S_EPS + 1], ACT.Ln)
                    values_out(p, 0)
                    act.wait_ge(proj_read, 8 * p + 6)
                    link(act.activation(sq, sq, ACT.Ln, bias=sm[:, S_EPS:S_EPS + 1], scale=1.0 / QK))
                    act.activation(sq, sq, ACT.Exp, scale=-0.5).then_inc(q_r, 1)
                elif what == "W":
                    split(U_PAIR + p + 2, halves=[a])
                elif what == "E":
                    values_out(p, 1)
                elif what == "S":
                    act.wait_ge(score_max, q + 1)
                    if p:
                        act.wait_ge(prob_t, q - 7)
                    act.activation(prob[a][:, tile_of(i)], s_bank(q)[:, 0:P * (i + 1)], ACT.Exp,
                                   bias=sm[:, S_NB + q % 8:S_NB + q % 8 + 1],
                                   scale=sm[:, S_SF + 4 * a + i:S_SF + 4 * a + i + 1],
                                   accum_out=sm[:, S_RS + q % 8:S_RS + q % 8 + 1]).then_inc(prob_exp, 1)
                elif what == "T":
                    act.wait_ge(prob_t, q + 1)
                    act.activation(pth[:, 0:i + 1, P * i:P * i + P],
                                   bank[5 + q % 2][:, 0:P * (i + 1)].rearrange("p (j q) -> p j q", q=P),
                                   ACT.Copy).then_inc(pt_hi, 1)
                elif what == "V":
                    act.wait_ge(pv, head + 1)
                    act.activation(mixh[:, 2 + head, :], bank[7][:, :], ACT.Copy).then_inc(mx_hi, 1)

            for k in range(4):
                for o in range(2):
                    act.wait_ge(out_read, 2 * (H_OOUT + k) + o + 1)
                    gx(2 * k + o, C_FFN + KC)
                split(U_OOUT + k + 2)
            ffn(U_F1, H_F1, 1, None)

        @block.vector
        def _(dve):
            links = [0]

            def link(ins):
                links[0] += 1
                ins.then_inc(dve_chain, 1)
                dve.wait_ge(dve_chain, links[0])

            def split(n, i=None, halves=(0, 1)):
                s = n % 2
                w = unit_width(n)
                for k in halves:
                    a, b = k * (w // 2), (k + 1) * (w // 2)
                    if i is None:
                        dve.wait_ge(split_hi, 2 * n + k + 1)
                    else:
                        dve.wait_ge(split_hi, 4 * i + 2 * n + k + 1)
                    dve.tensor_tensor(wl[s][:, a:b], raw[s][:, a:b], wh[s][:, a:b], ALU.subtract).then_inc(split_lo, 1)

            def gx(c, g, k):
                dve.wait_ge(gx_hi, k + c + 1)
                dve.scalar_tensor_tensor(out=gxl[:, c, :], in0=x[:, c, :], scalar=col(g + c), in1=gxh[:, c, :],
                                         op0=ALU.mult, op1=ALU.subtract).then_inc(gx_lo, 1)

            def out_bank(h, o):
                return bank[2 * (h % 2) + o]

            def wait_out(n, h, o):
                dve.wait_ge(half_ready, h + 1) if o == 0 else dve.wait_ge(unit_used, n + 1)

            def gate_step(n, h, i=None):
                k = 0 if i is None else 2 * i
                g = h - H_F0 if h < H_OIN else h - H_F1 + 2 * HC
                c = (g % HC) + k
                dve.wait_ge(half_ready, k + h + 1)
                if g:
                    dve.wait_ge(hid_lo, k + g)
                dve.tensor_tensor(gate_s[:], out_bank(h, 0)[:, :], rstd[:], ALU.mult).then_inc(out_read, 1)
                dve.wait_ge(unit_used, k + n + 1)
                dve.tensor_tensor(up_s[:], out_bank(h, 1)[:, :], rstd[:], ALU.mult).then_inc(out_read, 1)
                dve.wait_ge(silu_done, k + g + 1)
                dve.wait_ge(out_read, 2 * k + 2 * h + 2)
                dve.tensor_tensor(gate_s[:], gate_s[:], up_s[:], ALU.mult).then_inc(prod_done, 1)
                dve.wait_ge(hid_hi, k + g + 1)
                if i is None:
                    hi, lo = hidh[:, c, :], hidl[:, c, :]
                else:
                    hi = hidh[:, bass.ds(c, 1), :].rearrange("p a t -> p (a t)")
                    lo = hidl[:, bass.ds(c, 1), :].rearrange("p a t -> p (a t)")
                dve.tensor_tensor(lo, gate_s[:], hi, ALU.subtract).then_inc(hid_lo, 1)

            def rotate(src, swapped):
                for g in range(4):
                    a, b = 32 * g, 32 * (g ^ 1)
                    ins = dve.tensor_tensor(swapped[b:b + 32, :], src[a:a + 32, :], sinT[a:a + 32, :], ALU.mult)
                return ins

            def down_step(n, m, g, k, i=None):
                e = 0 if i is None else 2 * i
                dve.wait_ge(unit_used, e + n + 1)
                b = bank[4 + n % 2][:, :]
                if i is None:
                    xm, cm, hi, lo = x[:, m, :], None if g is None else col(g + m), gxh[:, m, :], gxl[:, m, :]
                else:
                    mm = e + m
                    xm = x[:, bass.ds(mm, 1), :].rearrange("p a t -> p (a t)")
                    hi = gxh[:, bass.ds(mm, 1), :].rearrange("p a t -> p (a t)")
                    lo = gxl[:, bass.ds(mm, 1), :].rearrange("p a t -> p (a t)")
                    cm = None if g is None else cols[:, bass.ds(g + mm, 1)]
                dve.tensor_tensor(xm, xm, b, ALU.add).then_inc(x_done, 1)
                if g is not None:
                    dve.wait_ge(gx_hi, e + k + m + 1)
                    dve.scalar_tensor_tensor(out=lo, in0=xm, scalar=cm, in1=hi,
                                             op0=ALU.mult, op1=ALU.subtract).then_inc(gx_lo, 1)

            def ffn(base, hbase, layer, gain_next):
                for half in range(2):
                    n, h = base + half * HALF_UNITS, hbase + half * HC
                    if half == 0:
                        dve.wait_ge(norm_done, 2 * layer + 3)
                    gate_step(n, h)
                    split(n + 2)
                    with dve.Fori(0, 4) as i:
                        for j in range(2):
                            gate_step(n + 1 + j, h + 1 + j, i)
                            split(n + 3 + j, i)
                    for c in range(9, 11):
                        gate_step(n + c, h + c)
                        split(n + c + 2)
                    g = gain_next if half == 1 else None
                    k = (2 * layer + 2) * KC
                    n += HC
                    with dve.Fori(0, 3) as i:
                        for j in range(2):
                            down_step(n + j, j, g, k, i)
                            split(n + 2 + j, i)
                    for m in range(6, 8):
                        down_step(n + m, m, g, k)
                        if n + m + 2 < N_UNITS:
                            split(n + m + 2)

            dve.memset(ones[:], 1.0)
            dve.memset(pwr[:], 0.0).then_inc(vconst, 1)
            dve.memset(sm[:, S_EPS:S_EPS + 1], EPS)
            for g in range(2):
                dve.memset(half_rows[64 * g:64 * g + 64, g:g + 1], 1.0)
                dve.memset(half_rows[64 * (1 - g):64 * (1 - g) + 64, g:g + 1], 0.0)
                dve.memset(head_ones[:, g, g:g + 1], 1.0)
                dve.memset(head_ones[:, g, 1 - g:2 - g], 0.0)
            dve.memset(z[:, 0:2], 0.0)
            for c in range(KC):
                gx(c, C_MIX, 0)
                if c < 4:
                    dve.wait_ge(split_hi if c % 2 else first_hi, c // 2 + 1)
                    quarter = slice(c * T, c * T + T)
                    dve.tensor_tensor(wl[0][:, quarter], raw[0][:, quarter], wh[0][:, quarter],
                                      ALU.subtract).then_inc(split_lo if c % 2 else first_lo, 1)
            split(1)
            dve.wait_ge(consts_landed, 16 * 8)
            link(dve.tensor_copy(ang[:], posi[:]))
            link(dve.tensor_scalar(ang[:], ang[:], col(C_INVF), None, ALU.mult))
            link(dve.tensor_scalar(turn[:], ang[:], 0.15915494309189535, 12582912.0, ALU.mult, ALU.add))
            link(dve.tensor_scalar(turn[:], turn[:], 12582912.0, None, ALU.subtract))
            for part in (6.28125, 0.001934051513671875, 1.2556659e-06):
                link(dve.scalar_tensor_tensor(out=ang[:], in0=turn[:], scalar=-part, in1=ang[:],
                                              op0=ALU.mult, op1=ALU.add))
            dve.tensor_scalar(ang[:], ang[:], 3.1415925, -3.1415925, ALU.min, ALU.max).then_inc(vconst, 1)
            dve.wait_ge(aconst, 1)
            link(dve.tensor_tensor(hsin[:], hsin[:], hsin[:], ALU.mult))
            dve.tensor_scalar(cosT[:], hsin[:], -2.0, 1.0, ALU.mult, ALU.add)
            for g in range(3):
                dve.tensor_scalar(sinT[32 * g:32 * g + 32, :], turn[32 * g:32 * g + 32, :], -1.0 if g % 2 else 1.0,
                                  None, ALU.mult)
            dve.tensor_scalar(sinT[96:P, :], turn[96:P, :], -1.0, None, ALU.mult).then_inc(vconst, 1)

            split(2)
            dve.wait_ge(aconst, 2)
            dve.tensor_tensor(wsl[:], wsr[:], wsh[:], ALU.subtract).then_inc(v_lo, 1)
            split(3)

            def v_norm_part(part):
                if part == 0:
                    dve.wait_ge(v_gelu, TT)
                    link(dve.tensor_reduce(sm[:, S_SUM:S_SUM + 16], g4, AX.X, ALU.add))
                    dve.tensor_scalar(sm[:, S_MEAN:S_MEAN + 16], sm[:, S_SUM:S_SUM + 16], 1.0 / P, None,
                                      ALU.mult).then_inc(v_mean, 1)
                elif part == 1:
                    dve.wait_ge(v_sq, 1)
                    link(dve.tensor_reduce(sm[:, S_SUM:S_SUM + 16], mixed[:].rearrange("p t (h d) -> p (t h) d", d=P),
                                           AX.X, ALU.add))
                    dve.tensor_scalar(sm[:, S_VAR:S_VAR + 16], sm[:, S_SUM:S_SUM + 16], 1.0 / P, None,
                                      ALU.mult).then_inc(v_stat, 1)
                elif part == 3:
                    dve.wait_ge(v_hi, 1)
                    dve.tensor_tensor(vnl[:], gv[:], vnh[:], ALU.subtract).then_inc(v_lo, 1)

            dve.wait_ge(norm_done, 1)
            nb = 0
            for k in range(2, 8):
                split(k + 2)
                for o in range(2):
                    q = 2 * (k - 2) + o
                    kind, j = EVEN_ORDER[q]
                    h = H_EIN + k - 2
                    wait_out(k, h, o)
                    src = out_bank(h, o)[:, :]
                    if kind == "c":
                        dve.tensor_tensor(cb[:], src, rstd[:], ALU.mult).then_inc(out_read, 1)
                    elif kind == "h":
                        dve.tensor_tensor(gate_s[:], src, rstd[:], ALU.mult).then_inc(out_read, 1)
                        dve.wait_ge(out_read, 2 * h + o + 1)
                        link(dve.tensor_tensor(z[:, 2:], gate_s[:], cb[:], ALU.mult))
                        taps = [cols[:, C_CONV + 3 * j + i:C_CONV + 3 * j + i + 1] for i in range(3)]
                        link(dve.tensor_scalar(y[:], z[:, 2:], taps[2], None, ALU.mult))
                        for i in (1, 0):
                            link(dve.scalar_tensor_tensor(out=y[:], in0=z[:, i:i + T], scalar=taps[i], in1=y[:],
                                                          op0=ALU.mult, op1=ALU.add))
                    else:
                        nb += 1
                        dve.tensor_tensor(gate_s[:], src, rstd[:], ALU.mult).then_inc(out_read, 1)
                        dve.wait_ge(out_read, 2 * h + o + 1)
                        dve.tensor_tensor(up_s[:], gate_s[:], y[:], ALU.mult).then_inc(mx_f, 1)
                        dve.wait_ge(mx_hi, nb)
                        dve.tensor_tensor(mixl[:, 4 + j, :], up_s[:], mixh[:, 4 + j, :],
                                          ALU.subtract).then_inc(mx_lo, 1)
                v_norm_part(k - 2)
            for h in range(4):
                dve.wait_ge(mix_mm, h + 1)
                dve.tensor_tensor(mixed[:, h, :].rearrange("p (n t) -> p n t", t=P),
                                  bank[4 + h][:, :].rearrange("p (n t) -> p n t", t=P),
                                  bbc[:, h:h + 1, :].broadcast_to([P, 4, P]), ALU.add).then_inc(mix_read, 1)
            for k in range(8, 10):
                for o in range(2):
                    j = 2 * (k - 8) + o
                    h = H_EIN + k - 2
                    wait_out(k, h, o)
                    dve.tensor_tensor(gate_s[:], out_bank(h, o)[:, :], rstd[:], ALU.mult).then_inc(out_read, 1)
                    dve.wait_ge(u_gelu, j + 1)
                    dve.wait_ge(mix_read, 4)
                    dve.tensor_tensor(up_s[:], gate_s[:], mixed[:, j, :], ALU.mult).then_inc(mx_f, 1)
                    dve.wait_ge(mx_hi, 5 + j)
                    dve.tensor_tensor(mixl[:, j, :], up_s[:], mixh[:, j, :], ALU.subtract).then_inc(mx_lo, 1)
                split(k + 2)

            def out_proj(base, hbase, g, k0):
                for k in range(4):
                    for o in range(2):
                        m = 2 * k + o
                        wait_out(base + k, hbase + k, o)
                        dve.tensor_tensor(x[:, m, :], x[:, m, :], out_bank(hbase + k, o)[:, :],
                                          ALU.add).then_inc(out_read, 1)
                        gx(m, g, k0)
                    split(base + k + 2)

            out_proj(U_EOUT, H_EOUT, C_FFN, KC)
            ffn(U_F0, H_F0, 0, C_MIX + KC)

            dve.wait_ge(norm_done, 4)
            for c in range(2):
                dve.memset(zp[c][:, 0:15], 0.0)
            dve.wait_ge(aconst, 3)
            dve.tensor_tensor(pwl[:], pwr[:], pwh[:], ALU.subtract).then_inc(pw_lo, 1)
            for k in range(4):
                for o in range(2):
                    i = 2 * k + o - 2
                    h = H_OIN + k
                    wait_out(U_OIN + k, h, o)
                    dst = zp[o][:, 15:] if i < 0 else lat[:, i, :]
                    dve.tensor_tensor(dst, out_bank(h, o)[:, :], rstd[:], ALU.mult).then_inc(out_read, 1)
                    if 0 <= i < QC + KVC:
                        dve.wait_ge(lat_hi, i + 1)
                        dve.scalar_tensor_tensor(out=latl[:, i, :], in0=lat[:, i, :], scalar=col(C_LAT + i),
                                                 in1=lath[:, i, :], op0=ALU.mult,
                                                 op1=ALU.subtract).then_inc(lat_lo, 1)
                split(U_OIN + k + 2)
                if k == 2:
                    for c in range(2):
                        dve.wait_ge(pooled_hi, c + 1)
                        dve.tensor_tensor(mixl[:, 2 + c, :], pm[c][:], mixh[:, 2 + c, :],
                                          ALU.subtract).then_inc(pooled_lo, 1)
            dve.wait_ge(out_read, 2 * H_OIN + 8)
            link(dve.tensor_scalar(rkg[:], lat[:, 5, :], col(C_KGR), None, ALU.mult))
            dve.tensor_tensor(rot[0][:], rkg[:], cosT[:], ALU.mult)
            link(rotate(rkg, rot[1]))

            twice = lambda c: sm[:, c:c + 4].rearrange("p (a t) -> p a t", a=1).broadcast_to([P, 2, 4])
            both = lambda ap: ap.rearrange("p (a t) -> p a t", a=2)

            def values_out(p, a):
                dve.wait_ge(proj_hi, 6 * p + 4 + 2 * a)
                for t in range(2):
                    tt = 2 * a + t
                    ins = dve.scalar_tensor_tensor(out=vl[:, tt, :],
                                                   in0=bank[(10 * p + 8 + a) % 3][:, t * 256:t * 256 + 256],
                                                   scalar=sm[:, S_LAT + 4 + tt:S_LAT + 5 + tt],
                                                   in1=vh[:, tt, :], op0=ALU.mult, op1=ALU.subtract)
                ins.then_inc(proj_read, 1)

            def invert_sum(q):
                dve.wait_ge(prob_exp, q + 1)
                c = q % 8
                dve.reciprocal(sm[:, S_RI + c:S_RI + c + 1], sm[:, S_RS + c:S_RS + c + 1]).then_inc(row_recip, 1)

            exped = None
            for what, a, i, p in maxima_first(pair_steps()):
                b = 10 * p
                head = 2 * p + a
                q = 4 * head + i
                src = bank[(b + a) % 3][:, :]
                kind = PROJ[a] if what == "P" else ""
                if exped is not None and what != "S":
                    invert_sum(exped)
                    exped = None
                if kind in ("k0", "k1"):
                    if p == 0 and kind == "k0":
                        dve.wait_ge(lat_mm, 1)
                        dve.tensor_tensor(rk[:], rot[0][:], rot[1][:], ALU.add).then_inc(rk_done, 1)
                        dve.wait_ge(lat_r, 1)
                    dve.wait_ge(proj, 9 * p + a + 1)
                    if p:
                        dve.wait_ge(pair_lo, 4 * p)
                    dve.tensor_tensor(kk[:, a - 1, :], src, rkv[:], ALU.mult).then_inc(proj_read, 1)
                    if p == 0 and kind == "k1":
                        dve.wait_ge(lat_r, 2)
                        link(dve.tensor_tensor(sm[:, S_RQ2:S_RQ2 + 4], sm[:, S_LAT:S_LAT + 4],
                                               sm[:, S_LAT:S_LAT + 4], ALU.mult))
                elif kind in ("q0", "q1"):
                    o = a // 3
                    dve.wait_ge(proj_hi, 6 * p + o + 1)
                    dve.scalar_tensor_tensor(out=qnl[:, o, :], in0=src, scalar=col(C_QG), in1=qnh[:, o, :],
                                             op0=ALU.mult, op1=ALU.subtract).then_inc(proj_read, 1)
                elif kind == "qr":
                    dve.wait_ge(proj_sq, 5 * p + 5)
                    if p == 0:
                        dve.wait_ge(lat_sq, 2)
                    dve.tensor_scalar(qx[:], src, col(C_QGR), None, ALU.mult).then_inc(proj_read, 1)
                    dve.wait_ge(proj_read, 8 * p + 5)
                    if p:
                        dve.wait_ge(prob_t, 8 * p)
                    link(rotate(qx, qswap))
                    dve.wait_ge(q_dir, p + 1)
                    dve.tensor_tensor(qx[:], qdir[:], qswap[:], ALU.add).then_inc(q_rot, 1)
                    if p == 0:
                        for c in range(2):
                            dve.wait_ge(mx_hi, KC + c + 1)
                            dve.scalar_tensor_tensor(out=mixl[:, c, :], in0=bank[3 + c][:, :],
                                                     scalar=col(C_PSCALE + c), in1=mixh[:, c, :], op0=ALU.mult,
                                                     op1=ALU.subtract).then_inc(mx_lo, 1)
                elif what == "F":
                    for o in range(2):
                        dve.wait_ge(k_r, 2 * p + o + 1)
                        dve.scalar_tensor_tensor(out=kk[:, o, :], in0=kk[:, o, :], scalar=col(C_KG),
                                                 in1=fk[:, o, :], op0=ALU.mult, op1=ALU.mult).then_inc(k_f, 1)
                        if o == 0:
                            dve.wait_ge(k_r, 2 * p + 2)
                            dve.tensor_tensor(krp[64:P, :], rk[64:P, :], fk[64:P, 1, :], ALU.mult).then_inc(kr_v, 1)
                    if p == 0:
                        dve.tensor_scalar(pth[:, 3, 2 * P:3 * P], ident[:], 0.0, None, ALU.mult)
                        dve.tensor_scalar(ptl[:, 3, 2 * P:3 * P], ident[:], 0.0, None, ALU.mult)
                elif what == "G":
                    dve.wait_ge(k_hi, 4 * p + 1)
                    dve.tensor_tensor(knl[:, 0, :], kk[:, 0, :], knh[:, 0, :], ALU.subtract).then_inc(pair_lo, 1)
                    dve.wait_ge(k_hi, 4 * p + 2)
                    dve.tensor_tensor(qrl[:], qx[:], qrh[:], ALU.subtract).then_inc(pair_lo, 1)
                    dve.wait_ge(k_hi, 4 * p + 3)
                    dve.tensor_tensor(krl[:], krp[:], krh[:], ALU.subtract).then_inc(pair_lo, 1)
                    dve.wait_ge(k_hi, 4 * p + 4)
                    dve.tensor_tensor(knl[:, 1, :], kk[:, 1, :], knh[:, 1, :], ALU.subtract).then_inc(pair_lo, 1)
                elif what == "Q":
                    dve.wait_ge(proj, 9 * p + 8)
                    if p:
                        dve.wait_ge(sf_done, p)
                    sums = bank[(b + 7) % 3][:, 0:8].rearrange("p (t a) -> p a t", a=2)
                    dve.tensor_tensor(both(sm[:, S_Q:S_Q + 8]), sums, twice(S_RQ2), ALU.mult).then_inc(proj_read, 1)
                    values_out(p, 0)
                    dve.wait_ge(q_r, p + 1)
                    dve.scalar_tensor_tensor(out=both(sm[:, S_SF:S_SF + 8]), in0=both(sm[:, S_Q:S_Q + 8]),
                                             scalar=SM_SCALE, in1=twice(S_LAT), op0=ALU.mult,
                                             op1=ALU.mult).then_inc(sf_done, 1)
                elif what == "W":
                    split(U_PAIR + p + 2, halves=[a])
                elif what == "E":
                    values_out(p, 1)
                elif what == "S":
                    dve.wait_ge(score, q + 1)
                    dve.wait_ge(sf_done, p + 1)
                    mx, nb = (sm[:, c + q % 8:c + q % 8 + 1] for c in (S_MX, S_NB))
                    link(dve.tensor_reduce(mx, s_bank(q)[:, 0:P * (i + 1)], AX.X, ALU.max))
                    dve.scalar_tensor_tensor(out=nb, in0=mx, scalar=-1.0,
                                             in1=sm[:, S_SF + 4 * a + i:S_SF + 4 * a + i + 1],
                                             op0=ALU.mult, op1=ALU.mult).then_inc(score_max, 1)
                    if exped is not None:
                        invert_sum(exped)
                    exped = q
                elif what == "T":
                    dve.wait_ge(pt_hi, q + 1)
                    dve.tensor_tensor(ptl[:, 0:i + 1, P * i:P * i + P],
                                      bank[5 + q % 2][:, 0:P * (i + 1)].rearrange("p (j q) -> p j q", q=P),
                                      pth[:, 0:i + 1, P * i:P * i + P], ALU.subtract).then_inc(pt_lo, 1)
                elif what == "V":
                    dve.wait_ge(mx_hi, KC + 2 + head + 1)
                    dve.tensor_tensor(mixl[:, 2 + head, :], bank[7][:, :], mixh[:, 2 + head, :],
                                      ALU.subtract).then_inc(mx_lo, 1)

            out_proj(U_OOUT, H_OOUT, C_FFN + KC, 3 * KC)
            ffn(U_F1, H_F1, 1, None)

        @block.tensor
        def _(pe):
            def mm3(dst, wa, wb, xa, xb, start, stop):
                pe.matmul(dst, wb, xa, start=start, stop=False)
                pe.matmul(dst, wa, xb, start=False, stop=False)
                return pe.matmul(dst, wa, xa, start=False, stop=stop)

            def arrived(n, i=None):
                if i is None:
                    pe.wait_ge(split_lo, 2 * (n + 1))
                else:
                    pe.wait_ge(split_lo, 4 * i + 2 * (n + 1))

            def two_out(n, h, xh_, xl_, order=range(KC), before=None):
                arrived(n)
                if h >= 2:
                    pe.wait_ge(out_read, 2 * (h - 1))
                s = n % 2
                for o in range(2):
                    for k, kc in enumerate(order):
                        if before:
                            before(o, kc)
                        a = (o * KC + kc) * P
                        ins = mm3(bank[2 * (h % 2) + o][:, :], wh[s][:, a:a + P], wl[s][:, a:a + P],
                                  xh_[:, kc, :], xl_[:, kc, :], k == 0, k == KC - 1)
                    ins.then_inc(half_ready if o == 0 else unit_used, 1)

            def norm(k):
                pe.wait_ge(sumsq, k)
                dst = bank[2] if k == 1 else bank[6]
                pe.matmul(dst[:, :], ones[:], acc[:], start=True, stop=True).then_inc(norm_mm, 1)

            def gate_body(n, h, i=None):
                s = n % 2
                for o in range(2):
                    for kc in range(KC):
                        a = (o * KC + kc) * P
                        ins = mm3(bank[2 * (h % 2) + o][:, :], wh[s][:, a:a + P], wl[s][:, a:a + P],
                                  gxh[:, kc, :], gxl[:, kc, :], kc == 0, kc == KC - 1)
                    ins.then_inc(half_ready if o == 0 else unit_used, 1)

            def down_body(n, m, g, done, i=None):
                arrived(n, i)
                if i is not None:
                    pe.wait_ge(x_done, 2 * i + done + m - 1)
                elif done:
                    pe.wait_ge(x_done, done)
                s = n % 2
                for kc in range(HC):
                    if kc in (0, HC - 1):
                        pe.wait_ge(hid_lo, g + HC - (kc == 0))
                    ks = slice(kc * P, kc * P + P)
                    ins = mm3(bank[4 + s][:, :], wh[s][:, ks], wl[s][:, ks], hidh[:, kc, :], hidl[:, kc, :],
                              kc == 0, kc == HC - 1)
                ins.then_inc(unit_used, 1)

            def ffn(base, hbase, layer):
                for half in range(2):
                    n, h = base + half * HALF_UNITS, hbase + half * HC
                    if half == 0:
                        two_out(n, h, gxh, gxl,
                                before=lambda o, kc: pe.wait_ge(gx_lo, (2 * layer + 1) * KC + kc + 1) if o == 0 else None)
                        norm(2 * layer + 2)
                    else:
                        two_out(n, h, gxh, gxl)
                    with pe.Fori(0, (HC - 1) // 2) as i:
                        for j in range(2):
                            arrived(n + 1 + j, i)
                            pe.wait_ge(out_read, 4 * i + 2 * (h + j))
                            gate_body(n + 1 + j, h + 1 + j)
                    n += HC
                    g = (2 * layer + half) * HC
                    for m in range(2):
                        down_body(n + m, m, g, (2 * layer + half) * KC)
                    with pe.Fori(0, KC // 2 - 1) as i:
                        for j in range(2):
                            down_body(n + 2 + j, 2 + j, g, (2 * layer + half) * KC, i)

            pe.wait_ge(vconst, 1)
            for k in range(WARM_UP):
                pe.matmul(bank[0][:, 0:P], ones[:], ones[:], start=True, stop=True)
            for n in range(2):
                for k in range(4):
                    kc = 4 * n + k
                    if n == 0 and k % 2 == 0:
                        pe.wait_ge(first_lo, k // 2 + 1)
                    else:
                        pe.wait_ge(split_lo, 2 * n + 1 + k // 2)
                    pe.wait_ge(gx_lo, kc + 1)
                    for t in range(TT):
                        a, b = k * T, k * T + T
                        ts = slice(t * P, t * P + P)
                        ins = mm3(bank[4 + t][:, :], gxh[:, kc, ts], gxl[:, kc, ts], wh[n][:, a:b], wl[n][:, a:b],
                                  kc == 0, kc == KC - 1)
                ins.then_inc(unit_used, 1)
            norm(1)
            for t in range(TT):
                ins = pe.matmul(bank[3][:, t:t + 1], acc[:, t * P:t * P + P], ones[:, 0:1], start=True, stop=True)
            ins.then_inc(norm_mm, 1)
            for k in range(2, 10):
                if k == 3:
                    pe.wait_ge(norm_done, 2)
                two_out(k, H_EIN + k - 2, gxh, gxl)
                if k == 7:
                    pe.wait_ge(v_lo, 2)
                    for h in range(4):
                        for c in range(TT):
                            hs, cs = slice(h * P, h * P + P), slice(c * P, c * P + P)
                            ins = mm3(bank[4 + h][:, cs], vnh[:, c, hs], vnl[:, c, hs], wsh[:, h, :], wsl[:, h, :],
                                      True, True)
                        ins.then_inc(mix_mm, 1)
            conv_first = [4, 5, 6, 7, 0, 1, 2, 3]
            for k in range(4):
                two_out(U_EOUT + k, H_EOUT + k, mixh, mixl, conv_first,
                        before=(lambda o, kc: pe.wait_ge(mx_lo, kc - 3 if kc > 3 else kc + 5) if o == 0 else None)
                        if k == 0 else None)
            ffn(U_F0, H_F0, 0)

            for k in range(4):
                two_out(U_OIN + k, H_OIN + k, gxh, gxl,
                        before=(lambda o, kc: pe.wait_ge(gx_lo, 2 * KC + kc + 1) if o == 0 else None)
                        if k == 0 else None)
                if k == 0:
                    norm(3)
            def latent_norms():
                pe.wait_ge(lat_sq, 1)
                pe.wait_ge(norm_done, 4)
                for a, src in ((0, acc), (4, acckv)):
                    for t in range(TT):
                        pe.matmul(bank[6][:, a + t:a + t + 1], src[:, t * P:t * P + P], ones[:, 0:1],
                                  start=True, stop=True)
                pe.matmul(bank[7][:, :], ones[:], acckv[:], start=True, stop=True).then_inc(lat_mm, 1)

            def pooling():
                pe.wait_ge(pw_lo, 1)
                pe.wait_ge(pooled_lo, 2)
                for c in range(2):
                    mm3(bank[3 + c][:, :], pwh[:, c, :], pwl[:, c, :], mixh[:, 2 + c, :], mixl[:, 2 + c, :],
                        True, True).then_inc(pool_mm, 1)

            def project(p, o):
                b = 10 * p
                s = (U_PAIR + p) % 2
                k_at = QC * 3 * P
                v_at = k_at + KVC * 2 * P
                dst = bank[(b + o) % 3]
                g = b + o - 3
                if g < 0:
                    pe.wait_ge(out_read, 2 * H_OOUT)
                elif PROJ[g % 10] in ("s0", "s1"):
                    pe.wait_ge(k_ln, 2 * (g // 10) + g % 10 - 4)
                else:
                    pe.wait_ge(proj_read, 8 * (g // 10) + (g % 10 + 1 if g % 10 < 5 else g % 10 - 1))
                kind = PROJ[o]
                if kind in ("q0", "q1", "qr"):
                    if o == 0:
                        arrived(U_PAIR + p)
                        pe.wait_ge(lat_lo, QC + KVC)
                    for kc in range(QC):
                        a = (kc * 3 + ("q0", "q1", "qr").index(kind)) * P
                        ins = mm3(dst[:, :], wh[s][:, a:a + P], wl[s][:, a:a + P],
                                  lath[:, kc, :], latl[:, kc, :], kc == 0, kc == QC - 1)
                elif kind in ("k0", "k1"):
                    for kc in range(KVC):
                        a = k_at + (kc * 2 + o - 1) * P
                        ins = mm3(dst[:, :], wh[s][:, a:a + P], wl[s][:, a:a + P],
                                  lath[:, QC + kc, :], latl[:, QC + kc, :], kc == 0, kc == KVC - 1)
                elif kind == "qs":
                    pe.wait_ge(proj_sq, 5 * p + 5)
                    for t in range(TT):
                        to = dst[:, 2 * t:2 * t + 2]
                        ts = slice(t * P, t * P + P)
                        for hd in range(2):
                            pe.matmul(to, sqq[:, hd, ts], head_ones[:, hd, :], start=hd == 0, stop=False)
                        ins = pe.matmul(to, sqr[:, ts], half_rows[:], start=False, stop=True)
                elif kind in ("s0", "s1"):
                    pe.wait_ge(k_sum, 2 * p + o - 4)
                    ins = pe.matmul(dst[:, :], ones[:], sqk[:, o - 5, :], start=True, stop=True)
                else:
                    for t in range(2):
                        tt = 2 * (o - 8) + t
                        ts = slice(tt * P, tt * P + P)
                        for kc in range(KVC):
                            a = v_at + kc * 2 * P
                            ins = mm3(dst[:, t * 256:t * 256 + 256], lath[:, QC + kc, ts], latl[:, QC + kc, ts],
                                      wh[s][:, a:a + 256], wl[s][:, a:a + 256], kc == 0, kc == KVC - 1)
                ins.then_inc(unit_used if kind == "v1" else proj, 1)

            def out_part(o, chunks, k=0):
                s = (U_OOUT + k) % 2
                for kc in chunks:
                    w = slice((o * KC + kc) * P, (o * KC + kc + 1) * P)
                    ins = mm3(bank[2 * ((H_OOUT + k) % 2) + o][:, :], wh[s][:, w], wl[s][:, w], mixh[:, kc, :],
                              mixl[:, kc, :], kc == 0, kc == KC - 1)
                return ins

            for what, a, i, p in pair_steps():
                head = 2 * p + a
                q = 4 * head + i
                N = P * (i + 1)
                ts = slice(i * P, i * P + P)
                if what == "P":
                    if p == 0 and PROJ[a] == "q1":
                        latent_norms()
                    if p == 0 and PROJ[a] == "qr":
                        pooling()
                    project(p, a)
                elif what == "S":
                    if i == 0:
                        pe.wait_ge(pair_lo, 4 * p + 3 + a)
                        if p == 0 and a == 0:
                            pe.wait_ge(mx_lo, KC + 2)
                    if q % 8 >= 4:
                        pe.wait_ge(prob_exp, q - 2 if q % 8 == 7 else q - 3)
                    elif q % 8 == 3:
                        pe.wait_ge(proj_read, 8 * p + 6)
                    elif q % 8 == 2 and p:
                        pe.wait_ge(mx_lo, KC + 2 + head)
                    elif p:
                        pe.wait_ge(prob_exp, 8 * p)
                    r = slice(64 * a, 64 * a + 64)
                    dst = s_bank(q)
                    W = max(N, 2 * P)
                    mm3(dst[:, 0:W], qnh[:, a, ts], qnl[:, a, ts], knh[:, a, 0:W], knl[:, a, 0:W], True, False)
                    mm3(dst[:, 0:W], qrh[r, ts], qrl[r, ts], krh[r, 0:W], krl[r, 0:W], False, False)
                    pe.matmul(dst[:, N - P:N], identb[:], maskb[:], start=False, stop=True).then_inc(score, 1)
                elif what == "T":
                    pe.wait_ge(prob_n, q + 1)
                    if q >= 2:
                        pe.wait_ge(pt_lo, q - 1)
                    else:
                        pe.wait_ge(lat_r, 2)
                    for j in range(i + 1):
                        at_ = tile_of(i).start + j * P
                        ins = pe.transpose(bank[5 + q % 2][:, j * P:j * P + P], prob[a][:, at_:at_ + P], ident[:])
                    ins.then_inc(prob_t, 1)
                elif what == "V":
                    pe.wait_ge(pt_lo, 4 * (head + 1))
                    pe.wait_ge(proj_read, 8 * (p + 1))
                    if a:
                        pe.wait_ge(mx_lo, KC + 2 + head)
                    else:
                        pe.wait_ge(prob_exp, 8 * p + 7)
                    for j in range(TT):
                        hs = slice(a * P, a * P + P)
                        q0 = min(j, TT - 2) * P
                        ins = mm3(bank[7][:, q0:T], vh[:, j, hs], vl[:, j, hs], pth[:, j, q0:T],
                                  ptl[:, j, q0:T], j == 0, j == TT - 1)
                    ins.then_inc(pv, 1)
                elif what == "O":
                    if a == 0:
                        arrived(U_OOUT)
                        pe.wait_ge(proj_read, 8 * PAIRS)
                        pe.wait_ge(mx_lo, KC + HEADS)
                        out_part(0, range(6))
                    elif a == 1:
                        out_part(1, range(5))
                    else:
                        out_part(1, [5])
                        pe.wait_ge(mx_lo, KC + HEADS + 1)
                        for o in range(2):
                            out_part(o, [6])
            arrived(U_OOUT + 1)
            out_part(0, range(3), 1)
            pe.wait_ge(mx_lo, 2 * KC)
            for o in range(2):
                out_part(o, [7]).then_inc(half_ready if o == 0 else unit_used, 1)
            out_part(0, range(3, KC), 1).then_inc(half_ready, 1)
            out_part(1, range(KC), 1).then_inc(unit_used, 1)
            for k in range(2, 4):
                two_out(U_OOUT + k, H_OOUT + k, mixh, mixl)
            ffn(U_F1, H_F1, 1)


def kernel(**inputs):
    import numpy as np
    import concourse.bacc as bacc
    from concourse.bass_utils import run_bass_kernel_spmd

    a = {k: np.asarray(v) for k, v in inputs.items()}

    def chunks(w):
        k, m = w.shape
        return w.reshape(k // P, P, m // P, P).transpose(2, 1, 0, 3).reshape(m // P, P, k)

    def pairs(c, order):
        return np.stack([np.concatenate([c[order[i]], c[order[i + 1]]], axis=1) for i in range(0, len(order), 2)])

    ein = a["even_w_in"][0]
    v_units = ein[:, 512:1024].reshape(2, 4, P, 512).transpose(0, 2, 1, 3).reshape(2, P, W_UNIT)
    c = chunks(ein)
    at = {"b": 8, "c": 12, "h": 16}
    w_ein = np.concatenate([v_units, pairs(c, [at[k] + j for k, j in EVEN_ORDER] + [0, 1, 2, 3])])
    w_eout = pairs(chunks(a["even_w_out"][0]), list(range(8)))
    oin = a["odd_w_in"][0]
    c = chunks(np.concatenate([oin, oin[:, -64:]], axis=1))
    w_oin = pairs(c, list(range(8)))
    w_oout = pairs(chunks(a["odd_w_out"][0]), list(range(8)))
    qb = a["q_b"][0].reshape(QC, P, HEADS, QK)
    kvb = a["kv_b"][0].reshape(KVC, P, HEADS, 2 * P)
    w_pair = []
    for h in range(0, HEADS, 2):
        q = np.concatenate([qb[:, :, h, :P], qb[:, :, h + 1, :P], qb[:, :, h, P:], qb[:, :, h + 1, P:]], axis=2)
        k = np.concatenate([kvb[:, :, h, :P], kvb[:, :, h + 1, :P]], axis=2)
        v = np.concatenate([kvb[:, :, h, P:], kvb[:, :, h + 1, P:]], axis=2)
        w_pair.append(np.concatenate([t.transpose(1, 0, 2).reshape(P, -1) for t in (q, k, v)], axis=1))
    w_pair = np.stack(w_pair)
    w_gu = np.stack([np.concatenate([chunks(a["ffn_w_gate"][l]), chunks(a["ffn_w_up"][l])], axis=2) for l in range(2)])
    w_dn = np.stack([np.concatenate([chunks(a["ffn_w_down"][l][h * HC * P:(h + 1) * HC * P]) for h in range(2)])
                     for l in range(2)])

    def columns(v):
        return v.reshape(-1, P).T

    conv = a["sc_conv_w"][0].reshape(3, 4, P).transpose(2, 1, 0).reshape(P, 12)
    twice = lambda v: np.concatenate([v, v])[:, None]
    qg, kg = a["q_norm"][0], a["k_norm"][0]
    freq = (10000.0 ** (-np.arange(0, 64, 2) / 64.0)).astype(np.float32)
    window = np.array([[2, 4], [8, 16]])
    row_window = np.repeat(window, 64, axis=1).T
    fix = row_window[:, :, None] / np.minimum(np.arange(1, 17)[None, None], row_window[:, :, None])
    cols = np.concatenate([
        columns(a["mix_norm"].reshape(-1)), columns(a["ffn_norm"].reshape(-1)), conv, columns(a["pool_scale"][0]),
        columns(a["q_a_norm"][0]), columns(a["kv_a_norm"][0]), qg[:P, None], twice(qg[P:]), kg[:P, None],
        twice(kg[P:]), np.tile(freq, 4)[:, None], (1.0 / row_window).astype(np.float32),
        fix.reshape(P, 32).astype(np.float32)], axis=1)

    arrays = {
        "xT": a["x"][0].T.reshape(KC, P, T).transpose(1, 0, 2),
        "pos": a["positions"],
        "cols": cols,
        "sg_g": a["sg_ln_g"],
        "sg_b": a["sg_b_s"].reshape(1, T),
        "sg_w": a["sg_w_s"][0].transpose(2, 0, 1),
        "pool_w": a["pool_w"][0],
        "w_ein": w_ein, "w_eout": w_eout, "w_oin": w_oin, "w_pair": w_pair, "w_oout": w_oout,
        "w_gu": w_gu, "w_dn": w_dn,
    }
    nc = bacc.Bacc("TRN2", target_bir_lowering=False, num_devices=1)
    feeds, args = {}, []
    for name, v in arrays.items():
        v = np.ascontiguousarray(v)
        feeds[f"in_{name}"] = v
        args.append(nc.dram_tensor(f"in_{name}", v.shape, mybir.dt.from_np(v.dtype), kind="ExternalInput").ap())
    args.append(nc.dram_tensor("out_T", (P, KC, T), F32, kind="ExternalOutput").ap())
    trunk(nc, *args)
    r = run_bass_kernel_spmd(nc, [feeds], core_ids=[0])
    return np.ascontiguousarray(r.results[0]["out_T"].transpose(1, 0, 2).reshape(D, T).T)[None]
```
